# Optimizing a Trainium2 kernel written in Bass

```python
import math
import jax, jax.numpy as jnp
from jax import lax
import numpy as np

D_MODEL = 1024
BATCH = 1
SEQ = 512
DEPTH = 2

N_MIXERS = 2
N_HEADS = 16
A_LATENT = 128
A_VHEAD = 64
IDX_HEADS = 8
IDX_DIM = 64
TOPK_MAX = 256
Q_BLOCK = 128
B_KV_HEADS = 2
B_HEAD_DIM = 64
WINDOW = 128
D_FF = ((8 * D_MODEL + 3 * 256 - 1) // (3 * 256)) * 256
REL_BUCKETS = 32
REL_MAX_DIST = 128
EPS = 1e-6

A_SIZES = [N_HEADS * A_LATENT, A_LATENT, IDX_HEADS * IDX_DIM, IDX_DIM, IDX_HEADS]
A_IN = sum(A_SIZES)
B_SIZES = [N_HEADS * B_HEAD_DIM, B_KV_HEADS * B_HEAD_DIM, B_KV_HEADS * B_HEAD_DIM]
B_IN = sum(B_SIZES)
N_A_LAYERS = (DEPTH + 1) // 2
N_B_LAYERS = DEPTH // 2

kernel_name = "hybrid_dsa_swa_sink_t5bias_swiglu"

def _split(proj, sizes):
    offs, o = [], 0
    for s in sizes[:-1]:
        o += s
        offs.append(o)
    return jnp.split(proj, offs, axis=-1)

def rms_norm(x, g):
    xf = x.astype(jnp.float32)
    y = xf * lax.rsqrt(jnp.mean(xf * xf, axis=-1, keepdims=True) + EPS)
    return (y * g.astype(jnp.float32)).astype(x.dtype)

def rel_bucket(rel):
    n = jnp.maximum(rel, 0)
    max_exact = REL_BUCKETS // 2
    nf = jnp.maximum(n, max_exact).astype(jnp.float32)
    large = max_exact + (jnp.log(nf / max_exact) / math.log(REL_MAX_DIST / max_exact)
                         * (REL_BUCKETS - max_exact)).astype(jnp.int32)
    large = jnp.minimum(large, REL_BUCKETS - 1)
    return jnp.where(n < max_exact, n, large)

def dsa_mixer(h, w_in, latent_g, w_uv, w_out, rel_bias):
    B, T, _ = h.shape
    H, R = N_HEADS, A_LATENT
    k_sel = min(TOPK_MAX, T // 4)
    nblk = T // Q_BLOCK
    q_lat, c_kv, q_idx, k_idx, w_idx = _split(h @ w_in, A_SIZES)
    q_lat = q_lat.reshape(B, T, H, R)
    q_idx = q_idx.reshape(B, T, IDX_HEADS, IDX_DIM)
    c_kv = rms_norm(c_kv, latent_g)
    w_idx = w_idx * (IDX_HEADS ** -0.5)

    def to_blocks(a):
        return jnp.moveaxis(a.reshape((B, nblk, Q_BLOCK) + a.shape[2:]), 1, 0)

    s_pos = jnp.arange(T)

    def block(args):
        i, qlb, qib, wib = args
        t_pos = i * Q_BLOCK + jnp.arange(Q_BLOCK)
        dots = jnp.einsum('bqjd,bsd->bqjs', qib, k_idx) * (IDX_DIM ** -0.5)
        score = jnp.einsum('bqj,bqjs->bqs', wib, jax.nn.relu(dots)).astype(jnp.float32)
        causal = s_pos[None, :] <= t_pos[:, None]
        score = jnp.where(causal[None], score, -jnp.inf)
        _, idx = lax.top_k(score, k_sel)
        valid = idx <= t_pos[None, :, None]
        kv = jax.vmap(lambda c, ix: c[ix])(c_kv, idx)
        logits = jnp.einsum('bqhr,bqkr->bhqk', qlb, kv).astype(jnp.float32) * (R ** -0.5)
        bias = rel_bias[rel_bucket(t_pos[None, :, None] - idx)]
        logits = logits + jnp.transpose(bias, (0, 3, 1, 2)).astype(jnp.float32)
        logits = jnp.where(valid[:, None], logits, -jnp.inf)
        p = jax.nn.softmax(logits, axis=-1).astype(kv.dtype)
        return jnp.einsum('bhqk,bqkr->bqhr', p, kv)

    o = lax.map(block, (jnp.arange(nblk), to_blocks(q_lat), to_blocks(q_idx), to_blocks(w_idx)))
    o = jnp.moveaxis(o, 0, 1).reshape(B, T, H, R)
    o = jnp.einsum('bthr,hrd->bthd', o, w_uv).reshape(B, T, H * A_VHEAD)
    return o @ w_out

def swa_mixer(h, w_in, b_in, sinks, w_out, b_out, rel_bias):
    B, T, _ = h.shape
    W, G, KV, Dh = WINDOW, N_HEADS // B_KV_HEADS, B_KV_HEADS, B_HEAD_DIM
    nb = T // W
    q, k, v = _split(h @ w_in + b_in, B_SIZES)
    q = q.reshape(B, nb, W, KV, G, Dh)
    k = k.reshape(B, nb, W, KV, Dh)
    v = v.reshape(B, nb, W, KV, Dh)

    def with_prev(a):
        prev = jnp.pad(a, ((0, 0), (1, 0), (0, 0), (0, 0), (0, 0)))[:, :-1]
        return jnp.concatenate([prev, a], axis=2)

    kk, vv = with_prev(k), with_prev(v)
    logits = jnp.einsum('bnqkgd,bnskd->bnkgqs', q, kk).astype(jnp.float32) * (Dh ** -0.5)
    rel = (W + jnp.arange(W))[:, None] - jnp.arange(2 * W)[None, :]
    in_win = (rel >= 0) & (rel < W)
    key_exists = (jnp.arange(nb)[:, None] * W + jnp.arange(2 * W)[None, :] - W) >= 0
    mask = in_win[None] & key_exists[:, None, :]
    bias = rel_bias[rel_bucket(rel)].reshape(W, 2 * W, KV, G)
    logits = logits + jnp.transpose(bias, (2, 3, 0, 1)).astype(jnp.float32)
    logits = jnp.where(mask[None, :, None, None], logits, -jnp.inf)
    sink = jnp.broadcast_to(sinks.reshape(KV, G)[None, None, :, :, None, None].astype(jnp.float32),
                            logits.shape[:-1] + (1,))
    p = jax.nn.softmax(jnp.concatenate([logits, sink], axis=-1), axis=-1)[..., :-1]
    o = jnp.einsum('bnkgqs,bnskd->bnqkgd', p.astype(vv.dtype), vv)
    return o.reshape(B, T, N_HEADS * Dh) @ w_out + b_out

def swiglu(h, w_gate_up, w_down):
    g, u = jnp.split(h @ w_gate_up, 2, axis=-1)
    return (jax.nn.silu(g) * u) @ w_down

def setup_inputs(seed: int = 0) -> dict:
    key = jax.random.key(seed)
    ks = jax.random.split(key, 20)
    f = jnp.float32

    def w(k, shape, fan_in):
        return jax.random.normal(k, shape, f) * (fan_in ** -0.5)

    def gain(k, shape):
        return 1.0 + 0.02 * jax.random.normal(k, shape, f)

    return {
        "x": jax.random.normal(ks[0], (BATCH, SEQ, D_MODEL), f),
        "rel_bias": 0.5 * jax.random.normal(ks[1], (REL_BUCKETS, N_HEADS), f),
        "attn_norm": gain(ks[2], (DEPTH, D_MODEL)),
        "ffn_norm": gain(ks[3], (DEPTH, D_MODEL)),
        "final_norm": gain(ks[4], (D_MODEL,)),
        "a_w_in": w(ks[5], (N_A_LAYERS, D_MODEL, A_IN), D_MODEL),
        "a_latent_norm": gain(ks[6], (N_A_LAYERS, A_LATENT)),
        "a_w_uv": w(ks[7], (N_A_LAYERS, N_HEADS, A_LATENT, A_VHEAD), A_LATENT),
        "a_w_out": w(ks[8], (N_A_LAYERS, N_HEADS * A_VHEAD, D_MODEL), N_HEADS * A_VHEAD),
        "b_w_in": w(ks[9], (N_B_LAYERS, D_MODEL, B_IN), D_MODEL),
        "b_b_in": 0.02 * jax.random.normal(ks[10], (N_B_LAYERS, B_IN), f),
        "b_sinks": 0.5 * jax.random.normal(ks[11], (N_B_LAYERS, N_HEADS), f),
        "b_w_out": w(ks[12], (N_B_LAYERS, N_HEADS * B_HEAD_DIM, D_MODEL), N_HEADS * B_HEAD_DIM),
        "b_b_out": 0.02 * jax.random.normal(ks[13], (N_B_LAYERS, D_MODEL), f),
        "ffn_w_gate_up": w(ks[14], (DEPTH, D_MODEL, 2 * D_FF), D_MODEL),
        "ffn_w_down": w(ks[15], (DEPTH, D_FF, D_MODEL), D_FF),
    }

def reference(x, rel_bias, attn_norm, ffn_norm, final_norm,
              a_w_in, a_latent_norm, a_w_uv, a_w_out,
              b_w_in, b_b_in, b_sinks, b_w_out, b_b_out,
              ffn_w_gate_up, ffn_w_down):
    for layer in range(DEPTH):
        j = layer // N_MIXERS
        h = rms_norm(x, attn_norm[layer])
        if layer % N_MIXERS == 0:
            x = x + dsa_mixer(h, a_w_in[j], a_latent_norm[j], a_w_uv[j], a_w_out[j], rel_bias)
        else:
            x = x + swa_mixer(h, b_w_in[j], b_b_in[j], b_sinks[j], b_w_out[j], b_b_out[j], rel_bias)
        h = rms_norm(x, ffn_norm[layer])
        x = x + swiglu(h, ffn_w_gate_up[layer], ffn_w_down[layer])
    return rms_norm(x, final_norm)


_drawn_inputs = setup_inputs


def setup_inputs(seed=0):
    import zlib

    import numpy as np

    out = dict(_drawn_inputs(seed))
    spreads = {}
    factors = {'ffn_norm': 2.842,
     'final_norm': 8.289,
     'a_latent_norm': 6.796,
     'b_b_in': 21.914,
     'b_sinks': 31.51,
     'b_b_out': 18.451}
    for name, (base, spread) in spreads.items():
        noise = np.random.default_rng([zlib.crc32(name.encode()), seed]).standard_normal(out[name].shape)
        drawn = base * np.exp(spread * noise) if base else spread * noise
        out[name] = __import__('jax').numpy.asarray(drawn.astype(out[name].dtype))
    for name, factor in factors.items():
        out[name] = (out[name] * factor).astype(out[name].dtype)
    return out
```

```python
from contextlib import ExitStack

import numpy as np

import concourse.bass as bass
from concourse import mybir

F32 = mybir.dt.float32
F32R = mybir.dt.float32r
ALU = mybir.AluOpType
ACT = mybir.ActivationFunctionType

P = 128
D = 1024
T = 512
DM = D // P
NB = T // P
FF = 2816
FT = FF // P
H = 16
R = 128
DH = 64
JI = 8
TOPK = 128
BUCKETS, MAX_DIST = 32, 128
EPS = 1e-6
BIG = 1e30
TAKEN = -3e38

A_CKV, A_QI, A_KI = H * R, H * R + R, H * R + R + JI * DH
OFF = [0, P, 3 * P, 6 * P]
CAUSAL = 10 * P
OFFB = [0, P, 3 * P, 5 * P]
WIN = 7 * P

C_ID, C_DUP, C_CAUSAL, C_WIN, C_HOT = 0, P, 2 * P, 3 * P, 5 * P
GLEN = 640
C_END = C_HOT + GLEN

S_A1, S_A2, S_AO, S_F0, S_D0 = 0, 3, 11, 15, 37
S_BK, S_BQ, S_BO, S_F1, S_D1, S_END = 53, 54, 58, 62, 84, 100
U_A1, U_A2, U_AO, U_F0, U_D0 = 0, 6, 22, 30, 74
U_BK, U_BQ, U_BO, U_F1, U_D1, U_END = 90, 92, 100, 108, 152, 168
SLOT = 2048
KD = FT // 2
CUT_WIDE, CUT_DOWN = (1024, 2048), (768, KD * P)


def units_through(n):
    for s0, u0, per in ((S_D1, U_D1, 1), (S_F1, U_F1, 2), (S_BO, U_BO, 2), (S_BQ, U_BQ, 2),
                        (S_BK, U_BK, 2), (S_D0, U_D0, 1), (0, 0, 2)):
        if n >= s0:
            return u0 + per * (n - s0 + 1)


def held(engine, value):
    if isinstance(value, int):
        return value
    value = engine.snap(value)
    engine.to_reg(value)
    return value


def is_down(n):
    return S_D0 <= n < S_BK or n >= S_D1


def tables():
    t = np.zeros((P, C_END), np.float32)
    i = np.arange(P)
    t[:, C_ID:C_ID + P] = np.eye(P)
    t[:DH, C_DUP:C_DUP + P] = (i[None, :] % DH == i[:DH, None])
    t[:, C_CAUSAL:C_CAUSAL + P] = np.where(i[None, :] <= i[:, None], 0, BIG)
    rel = P + i[:, None] - np.arange(2 * P)[None, :]
    t[:, C_WIN:C_WIN + 2 * P] = np.where((rel >= 0) & (rel < P), 0, BIG)
    dist = np.maximum(T - 1 - np.arange(GLEN), 0)
    exact = BUCKETS // 2
    large = exact + (np.log(np.maximum(dist, exact) / exact) / np.log(MAX_DIST / exact)
                     * (BUCKETS - exact) + 1e-9).astype(np.int64)
    bucket = np.where(dist < exact, dist, np.minimum(large, BUCKETS - 1))
    t[:BUCKETS, C_HOT:C_HOT + GLEN] = np.where(bucket[None, :] == np.arange(BUCKETS)[:, None], -1, 0)
    return t


def trunk(nc, x_in, rel_bias, attn_norm, ffn_norm, final_norm, a_w_in, a_latent_norm, a_w_uv,
          a_w_out, b_w_in, b_b_in, b_sinks, b_w_out, b_b_out, w_gate_up, w_down, consts,
          bias_row, bias_toep, out):
    ctx = ExitStack()
    with ctx:
        def sb(name, shape, dt=F32, where=ctx):
            return where.enter_context(nc.sbuf_tensor(name, shape, dt))

        def sem(name):
            return ctx.enter_context(nc.semaphore(name))

        x = sb("x", [P, DM, T])
        xs_hi = sb("xs_hi", [P, DM * T], F32R)
        xs_lo = sb("xs_lo", [P, DM * T], F32R)
        raw = sb("raw", [P, 2, SLOT])
        w_hi = sb("w_hi", [P, 2, SLOT], F32R)
        w_lo = sb("w_lo", [P, 2, SLOT], F32R)
        tab = sb("tab", [P, C_HOT])
        params = sb("params", [P, 59])
        ones = sb("ones", [P, P])
        eps = sb("eps", [P, 1])
        spare = sb("spare", [P, 1])
        sq = sb("sq", [P, 2, T])
        ss = sb("ss", [P, T])
        std = sb("std", [P, T])
        rstd = sb("rstd", [P, T])

        am = ExitStack()
        q_all = sb("q_all", [P, H, T], F32, am)
        q_hi = sb("q_hi", [P, 2, T], F32R, am)
        q_lo = sb("q_lo", [P, 2, T], F32R, am)
        toep = sb("toep", [P, 2, T], F32, am)
        work = sb("work", [P, CAUSAL - P], F32, am)
        top8 = sb("top8", [P, 3, 8], F32, am)
        bm = sb("bm", [P, CAUSAL], F32, am)
        cT_hi = sb("cT_hi", [P, T], F32R, am)
        cT_lo = sb("cT_lo", [P, T], F32R, am)
        c_hi = sb("c_hi", [P, NB, R], F32R, am)
        c_lo = sb("c_lo", [P, NB, R], F32R, am)
        oT_hi = sb("oT_hi", [P, DM, T], F32R, am)
        oT_lo = sb("oT_lo", [P, DM, T], F32R, am)
        uv_raw = sb("uv_raw", [P, 2, DH], F32, am)
        uv_hi = sb("uv_hi", [P, 2, P], F32R, am)
        uv_lo = sb("uv_lo", [P, 2, P], F32R, am)
        w_col = sb("w_col", [P, 3, JI], F32, am)
        low = sb("low", [P, 2, NB], F32, am)
        rsum = sb("rsum", [P, 2, NB], F32, am)
        rinv = sb("rinv", [P, 2, NB], F32, am)
        am.close()
        x_tok = q_all[:, 0:DM, :].rearrange("p a b -> p (a b)").rearrange("p (t n) -> p t n", t=NB)
        hot = q_all[0:BUCKETS, 8:10, :].rearrange("p a b -> p (a b)")[:, 0:GLEN]
        rel_sb = q_all[0:BUCKETS, 10, 0:H]
        g_sb = q_all[0:H, 11:13, :].rearrange("p a b -> p (a b)")[:, 0:GLEN]
        par_rows = q_all[0:59, 13, 0:P]
        qi_hi, qi_lo = oT_hi[:, 0:4, :], oT_lo[:, 0:4, :]
        ki_hi, ki_lo = oT_hi[:, 4, :], oT_lo[:, 4, :]
        kw = bm[:, 0:T]
        c_raw = bm[:, T:2 * T]
        c_nrm = sq[:, 1, :]
        relu = q_all
        prob = raw[:, :, :].rearrange("p s n -> p (s n)")[:, 0:2 * CAUSAL].rearrange("p (s n) -> p s n", s=2)
        pt_hi = xs_hi[:, 0:2 * CAUSAL].rearrange("p (s n) -> p s n", s=2)
        pt_lo = xs_lo[:, 0:2 * CAUSAL].rearrange("p (s n) -> p s n", s=2)
        o_hi = xs_hi[:, 2 * CAUSAL:2 * CAUSAL + 2 * T].rearrange("p (s n) -> p s n", s=2)
        o_lo = xs_lo[:, 2 * CAUSAL:2 * CAUSAL + 2 * T].rearrange("p (s n) -> p s n", s=2)

        bmem = ExitStack()
        bq_all = sb("bq_all", [P, DM, T], F32, bmem)
        bq_raw = sb("bq_raw", [P, 2, T], F32, bmem)
        bq_hi = sb("bq_hi", [P, 2, T], F32R, bmem)
        bq_lo = sb("bq_lo", [P, 2, T], F32R, bmem)
        kv = sb("kv", [P, 2, T], F32, bmem)
        bk_hi = sb("bk_hi", [P, T], F32R, bmem)
        bk_lo = sb("bk_lo", [P, T], F32R, bmem)
        v_hi = sb("v_hi", [P, 2, NB, P], F32R, bmem)
        v_lo = sb("v_lo", [P, 2, NB, P], F32R, bmem)
        b_toep = sb("b_toep", [P, 2, 2, 2 * P], F32, bmem)
        b_bm = sb("b_bm", [P, 2, 2, 2 * P], F32, bmem)
        b_prob = sb("b_prob", [P, 2, 2, WIN], F32, bmem)
        bo_hi = sb("bo_hi", [P, DM, T], F32R, bmem)
        bo_lo = sb("bo_lo", [P, DM, T], F32R, bmem)
        sink = sb("sink", [P, H], F32, bmem)
        nsink = sb("nsink", [P, H], F32, bmem)
        nq_bias = sb("nq_bias", [P, DM], F32, bmem)
        sink2 = sb("sink2", [P, 2, 2], F32, bmem)
        nsink2 = sb("nsink2", [P, 2, 2], F32, bmem)
        b_low = sb("b_low", [P, 2, 2, NB], F32, bmem)
        b_rsum = sb("b_rsum", [P, 2, 2, NB], F32, bmem)
        b_sinkp = sb("b_sinkp", [P, 2, 2, NB], F32, bmem)
        b_rinv = sb("b_rinv", [P, 2, 2, NB], F32, bmem)
        bmem.close()
        bpt_hi = xs_hi[:, 0:2 * WIN].rearrange("p (s n) -> p s n", s=2)
        bpt_lo = xs_lo[:, 0:2 * WIN].rearrange("p (s n) -> p s n", s=2)

        fm = ExitStack()
        act_hi = sb("act_hi", [P, FT, T], F32R, fm)
        act_lo = sb("act_lo", [P, FT, T], F32R, fm)
        gate = sb("gate", [P, T], F32, fm)
        up = sb("up", [P, T], F32, fm)
        silu = sb("silu", [P, T], F32, fm)
        glu = sb("glu", [P, 2, T], F32, fm)
        fm.close()
        ym = ExitStack()
        y_t = sb("y_t", [P, DM, T], F32, ym)
        y_tok = sb("y_tok", [P, NB, D], F32, ym)
        ym.close()

        ps = ctx.enter_context(nc.psum_tensor("ps", [P, 8, T], F32))

        ident = tab[:, C_ID:C_ID + P]
        dup = tab[0:DH, C_DUP:C_DUP + P]
        causal = tab[:, C_CAUSAL:C_CAUSAL + P]
        window = tab[:, C_WIN:C_WIN + 2 * P]
        G_ATTN, G_FFN, G_FINAL, B_IN, B_OUT, G_LAT = (0, 8), (16, 24), 32, 40, 50, 58
        GAIN = [G_ATTN[0], G_FFN[0], G_ATTN[1], G_FFN[1]]

        raw_full = [sem("raw_full0"), sem("raw_full1")]
        hi_done, lo_done = sem("hi_done"), sem("lo_done")
        unit_done = sem("unit_done")
        tab_in, x_in_s, small_in, sink_in = sem("tab_in"), sem("x_in"), sem("small_in"), sem("sink_in")
        hot_in = sem("hot_in")
        set_up = sem("set_up")
        x_tr = sem("x_tr")
        x_new = sem("x_new")
        sq_done = sem("sq_done")
        ss_done = sem("ss_done")
        xhi_done, xlo_done = sem("xhi_done"), sem("xlo_done")
        ss_zero = sem("ss_zero")
        ss_sum = sem("ss_sum")
        std_done, rstd_done = sem("std_done"), sem("rstd_done")
        par_t, par_done = sem("par_t"), sem("par_done")
        g_mm, g_done, row_out, toep_out = sem("g_mm"), sem("g_done"), sem("row_out"), sem("toep_out")
        kw_done, ki_dup, ki_h, ki_l, w_tr, w_done = (sem(n) for n in
                                                     ("kw_done", "ki_dup", "ki_h", "ki_l", "w_tr", "w_done"))
        qi_h, qi_l = sem("qi_h"), sem("qi_l")
        dots, relu_done, acc_done, acc_zero = sem("dots"), sem("relu_done"), sem("acc_done"), sem("acc_zero")
        craw_done, csq_done, css_sum, cstd_done, crstd_done, cn_done = (
            sem(n) for n in ("craw_done", "csq_done", "css_sum", "cstd_done", "crstd_done", "cn_done"))
        cT_h, cT_l, c_tr, c_h, c_l = (sem(n) for n in ("cT_h", "cT_l", "c_tr", "c_h", "c_l"))
        qa_done = sem("qa_done")
        topk = sem("topk")
        mask_done = sem("mask_done")
        toep_full = [sem("toep_full0"), sem("toep_full1")]
        uv_full = [sem("uv_full0"), sem("uv_full1")]
        qh_done, ql_done = sem("qh_done"), sem("ql_done")
        bias_done = sem("bias_done")
        lg_done = sem("lg_done")
        neg_done = sem("neg_done")
        exp_done = sem("exp_done")
        rinv_done, nrm_done = sem("rinv_done"), sem("nrm_done")
        pt_done, pth_done, ptl_done = sem("pt_done"), sem("pth_done"), sem("ptl_done")
        o_done, oh_done, ol_done = sem("o_done"), sem("oh_done"), sem("ol_done")
        uvh_done, uvl_done, uv_done = sem("uvh_done"), sem("uvl_done"), sem("uv_done")
        oTh_done, oTl_done = sem("oTh_done"), sem("oTl_done")
        gate_done, up_done, silu_done, glu_done, ah_done, al_done = (
            sem(n) for n in ("gate_done", "up_done", "silu_done", "glu_done", "ah_done", "al_done"))
        kvr_done, kvb_done, bkh_done, bkl_done, v_tr, vh_done, vl_done, pad_done = (
            sem(n) for n in ("kvr_done", "kvb_done", "bkh_done", "bkl_done", "v_tr", "vh_done", "vl_done", "pad_done"))
        sink_done, nqb_done, bqr_done, bqa_done = sem("sink_done"), sem("nqb_done"), sem("bqr_done"), sem("bqa_done")
        btoep_full = [sem("btoep_full0"), sem("btoep_full1")]
        bqh_done, bql_done, bbias_done, blg_done, bneg_done, bexp_done = (
            sem(n) for n in ("bqh_done", "bql_done", "bbias_done", "blg_done", "bneg_done", "bexp_done"))
        bsinkp_done, bsink2_done, brs_done, brinv_done, bnrm_done = (
            sem(n) for n in ("bsinkp_done", "bsink2_done", "brs_done", "brinv_done", "bnrm_done"))
        bpt_done, bpth_done, bptl_done, bo_done, boh_done, bol_done = (
            sem(n) for n in ("bpt_done", "bpth_done", "bptl_done", "bo_done", "boh_done", "bol_done"))
        y_done, y_tr, ytok_done, out_done = sem("y_done"), sem("y_tr"), sem("ytok_done"), sem("out_done")
        TAB = 16

        def xs(buf, k):
            return buf[:, k * T:(k + 1) * T]

        def pieces(buf, n):
            if S_BQ <= n < S_BO:
                if buf is raw:
                    v = buf[:, n % 2, :].rearrange("p (k a j c) -> p a k j c", k=DM, a=2, j=2)
                else:
                    v = buf[:, n % 2, :].rearrange("p (k j a c) -> p a k j c", k=DM, a=2, j=2)
                return [v[:, a, :, :, :] for a in range(2)]
            cut = CUT_DOWN if is_down(n) else CUT_WIDE
            return [buf[:, n % 2, 0:cut[0]], buf[:, n % 2, cut[0]:cut[1]]]

        block = ctx.enter_context(nc.Block())

        @block.sync
        def _(sp):
            def slab(n, it, src):
                for dst, s in src(n % 2):
                    if n >= 2:
                        sp.wait_ge(lo_done, 2 * (n - 1) + 4 * it)
                    sp.dma_start(dst, s).then_inc(raw_full[n % 2], 16)

            def wide(w, c0):
                def src(slot):
                    v = raw[:, slot, :].rearrange("p (k n) -> p k n", k=DM)
                    g = w.rearrange("(k p) n -> p k n", p=P)
                    return [(v[:, 4 * i:4 * i + 4, :], g[:, 4 * i:4 * i + 4, bass.ds(c0, 256)])
                            for i in range(2)]
                return src

            def two_halves(w, c0, c1):
                def src(slot):
                    v = raw[:, slot, :].rearrange("p (k n) -> p k n", k=DM)
                    g = w.rearrange("(k p) n -> p k n", p=P)
                    return [(v[:, :, 0:P], g[:, :, bass.ds(c0, P)]),
                            (v[:, :, P:2 * P], g[:, :, bass.ds(c1, P)])]
                return src

            def down(w, c, m):
                def src(slot):
                    v = raw[:, slot, 0:KD * P].rearrange("p (k n) -> p k n", k=KD)
                    g = w.rearrange("(k p) n -> p k n", p=P)
                    return [(v[:, a:b, :], g[:, c * KD + a:c * KD + b, bass.ds(m * P, P)])
                            for a, b in ((0, 6), (6, KD))]
                return src

            def feed_forward(layer, s_gu, s_d):
                w = w_gate_up[layer]
                with sp.Fori(0, FT // 2) as i:
                    for v in range(2):
                        slab(s_gu + v, i, two_halves(w, (2 * i + v) * P, (2 * i + v) * P + FF))
                with sp.Fori(0, DM) as m:
                    for c in range(2):
                        slab(s_d + c, m, down(w_down[layer], c, m))

            sp.dma_start(tab[:, :], consts[:, 0:C_HOT]).then_inc(tab_in, 16)
            r0 = raw[:, 0, :].rearrange("p (k n) -> p k n", k=DM)
            aw = a_w_in[0].rearrange("(k p) n -> p k n", p=P)
            sp.dma_start(r0[:, :, 0:DH + JI], aw[:, :, A_KI:A_KI + DH + JI]).then_inc(raw_full[0], 16)
            sp.dma_start(r0[:, :, P:2 * P], aw[:, :, A_CKV:A_CKV + R]).then_inc(raw_full[0], 16)
            slab(1, 0, wide(a_w_in[0], A_QI))
            sp.wait_ge(g_done, 2)
            sp.dma_start(bias_row, g_sb).then_inc(row_out, 16)
            slab(2, 0, wide(a_w_in[0], A_QI + 256))
            sp.wait_ge(row_out, 16)
            skew = bass.AP(tensor=bias_row.tensor, offset=P - 1, ap=[[GLEN, H], [-1, P], [1, T]])
            sp.dma_start(bias_toep, skew).then_inc(toep_out, 16)
            with sp.Fori(0, 4) as i:
                for v in range(2):
                    slab(S_A2 + v, i, wide(a_w_in[0], (2 * i + v) * 256))
            sp.wait_ge(toep_out, 16)

            def toep_in(h, par, first=False):
                if not first:
                    sp.wait_ge(bias_done, 4 * (h - 1))
                sp.dma_start(toep[:, par, :], bias_toep[h]).then_inc(toep_full[par], 16)

            def uv_in(h, par, first=False):
                if not first:
                    sp.wait_ge(uvl_done, h - 1)
                sp.dma_start(uv_raw[:, par, :], a_w_uv[0, h]).then_inc(uv_full[par], 16)

            for h in range(2):
                toep_in(h, h, True)
                uv_in(h, h, True)
            for n in range(S_AO, S_AO + 2):
                slab(n, 0, wide(a_w_out[0], (n - S_AO) * 256))
            toep_in(2, 0)
            toep_in(3, 1)
            with sp.Fori(2, H // 2) as i:
                for v in range(2):
                    toep_in(2 * i + v, v)
                    uv_in(2 * i + v - 2, v)
            uv_in(H - 2, 0)
            uv_in(H - 1, 1)
            sp.wait_ge(ptl_done, 3 * H)
            for n in range(S_AO + 2, S_F0):
                slab(n, 0, wide(a_w_out[0], (n - S_AO) * 256))
            feed_forward(0, S_F0, S_D0)
            slab(S_BK, 0, wide(b_w_in[0], H * DH))
            sp.wait_ge(unit_done, U_BK)
            sp.dma_start(sink[:, :], b_sinks[0:1, :].broadcast_to([P, H])).then_inc(sink_in, 16)

            for n in range(S_BQ, S_BO):
                c0 = (n - S_BQ) * 2 * DH
                slab(n, 0, two_halves(b_w_in[0], c0, c0 + H // 2 * DH))

            def pair_in(j, par, first):
                for a in range(2):
                    if not first:
                        sp.wait_ge(bbias_done, 2 * (j - 1))
                    sp.dma_start(b_toep[:, par, a, :], bias_toep[j + a * (H // 2), :, T - 2 * P:T])\
                        .then_inc(btoep_full[par], 16)

            pair_in(0, 0, True)
            pair_in(1, 1, True)

            def bo_slab(n):
                v = raw[:, n % 2, :].rearrange("p (k n) -> p k n", k=DM)
                c0 = (n - S_BO) * 256
                for a in range(2):
                    sp.wait_ge(lo_done, 2 * (n - 1))
                    sp.dma_start(v[a * DH:(a + 1) * DH, :, :],
                                 b_w_out[0, a * 512:(a + 1) * 512, c0:c0 + 256]
                                 .rearrange("(k p) n -> p k n", p=DH)).then_inc(raw_full[n % 2], 16)

            for n in range(S_BO, S_F1):
                bo_slab(n)
            with sp.Fori(1, DM // 2) as i:
                for v in range(2):
                    pair_in(2 * i + v, v, False)
            feed_forward(1, S_F1, S_D1)
            for t in range(NB):
                sp.wait_ge(ytok_done, 2 * t + 2)
                sp.dma_start(out[0, t * P:(t + 1) * P, :], y_tok[:, t, :]).then_inc(out_done, 16)
            sp.wait_ge(out_done, 16 * NB)

        @block.gpsimd
        def _(pool):
            def split_lo(n, it=0):
                for half in range(2):
                    pool.wait_ge(hi_done, 2 * n + half + 1 + 4 * it)
                    nc.gpsimd.tensor_tensor(pieces(w_lo, n)[half], pieces(raw, n)[half],
                                            pieces(w_hi, n)[half].bitcast(F32), ALU.subtract)\
                        .then_inc(lo_done, 1)

            nc.gpsimd.memset(ones[:, :], 1.0).then_inc(set_up, 1)
            nc.gpsimd.memset(eps[:, :], EPS).then_inc(set_up, 1)
            nc.gpsimd.memset(ss[:, :], 0.0).then_inc(set_up, 1)
            nc.gpsimd.memset(raw[:, 0, :].rearrange("p (k n) -> p k n", k=DM)[:, :, DH + JI:P], 0.0)\
                .then_inc(set_up, 1)
            nc.gpsimd.memset(work[:, :], 0.0).then_inc(set_up, 1)
            nc.gpsimd.memset(uv_hi[:, :, :].bitcast(F32), 0.0).then_inc(set_up, 1)
            nc.gpsimd.memset(uv_lo[:, :, :].bitcast(F32), 0.0).then_inc(set_up, 1)
            pool.wait_ge(tab_in, TAB)
            pool.wait_ge(set_up, 5)
            for i in range(1, NB):
                d = OFF[i] - P + i * P
                nc.gpsimd.tensor_tensor(work[:, d:d + P], work[:, d:d + P], causal, ALU.subtract)\
                    .then_inc(acc_zero, 1)
            for n in range(S_A2 + 2):
                split_lo(n)
            with pool.Fori(0, 4) as i:
                for v in range(2):
                    split_lo(S_A2 + 2 + v, i)

            def head(hh, it=0):
                h, par = hh + 2 * it, hh % 2
                if hh < H:
                    n0 = held(pool, h + 1)
                    pool.wait_ge(tab_in, TAB)
                    pool.wait_ge(qh_done, n0)
                    nc.gpsimd.tensor_tensor(q_lo[:, par, :], q_all[:, h, :],
                                            q_hi[:, par, :].bitcast(F32), ALU.subtract).then_inc(ql_done, 1)
                    for i in range(NB):
                        n = (i + 1) * P
                        mask = causal if i == 0 else work[:, OFF[i] - P:OFF[i] - P + n]
                        if i == 0:
                            n0 = held(pool, 16 * (hh // 2 + 1 + it))
                            pool.wait_ge(mask_done, 3)
                            pool.wait_ge(toep_full[par], n0)
                        if hh > 0:
                            pool.wait_ge(neg_done, 4 * h - 3 + i)
                        nc.gpsimd.tensor_tensor(bm[:, OFF[i]:OFF[i] + n], toep[:, par, T - n:T], mask, ALU.add)\
                            .then_inc(bias_done, 1)
                if hh >= 3:
                    c0, p1 = (1 - par) * DH, 1 - par
                    pool.wait_ge(uvh_done, h - 2)
                    nc.gpsimd.tensor_tensor(uv_lo[:, p1, c0:c0 + DH], uv_raw[:, p1, :],
                                            uv_hi[:, p1, c0:c0 + DH].bitcast(F32), ALU.subtract)\
                        .then_inc(uvl_done, 1)

            for hh in range(4):
                head(hh)
            with pool.Fori(0, (H - 4) // 2) as i:
                head(4, i)
                head(5, i)
            for hh in range(H, H + 3):
                head(hh)
            for n in range(S_AO + 2, S_F0 + 2):
                split_lo(n)

            def feed_forward(s_gu, s_d):
                with pool.Fori(0, (FT - 2) // 2) as i:
                    for v in range(2):
                        split_lo(s_gu + 2 + v, i)
                split_lo(s_d)
                split_lo(s_d + 1)
                with pool.Fori(0, (2 * DM - 2) // 2) as i:
                    for v in range(2):
                        split_lo(s_d + 2 + v, i)

            feed_forward(S_F0, S_D0)
            split_lo(S_BK)
            split_lo(S_BK + 1)
            pool.wait_ge(unit_done, U_BK)
            nc.gpsimd.memset(v_hi[:, :, :, :].bitcast(F32), 0.0).then_inc(pad_done, 1)
            nc.gpsimd.memset(v_lo[:, :, :, :].bitcast(F32), 0.0).then_inc(pad_done, 1)
            for n in range(S_BQ + 1, S_BO + 2):
                split_lo(n)

            def pair(j, par, it):
                n0 = held(pool, j + 1)
                pool.wait_ge(tab_in, TAB)
                pool.wait_ge(bqh_done, n0)
                nc.gpsimd.tensor_tensor(bq_lo[:, par, :], bq_all[:, j, :],
                                        bq_hi[:, par, :].bitcast(F32), ALU.subtract).then_inc(bql_done, 1)
                for a in range(2):
                    if not (isinstance(j, int) and j < 2):
                        pool.wait_ge(bneg_done, 8 * (j - 1))
                    pool.wait_ge(btoep_full[par], 32 * (it + 1))
                    nc.gpsimd.tensor_tensor(b_bm[:, par, a, :], b_toep[:, par, a, :], window, ALU.add)\
                        .then_inc(bbias_done, 1)

            pair(0, 0, 0)
            pair(1, 1, 0)
            with pool.Fori(1, DM // 2) as i:
                for v in range(2):
                    pair(2 * i + v, v, i)
            for n in range(S_BO + 2, S_F1 + 2):
                split_lo(n)
            feed_forward(S_F1, S_D1)

        @block.tensor
        def _(pe):
            def mm3(dst, wh, wl, xh, xl, start, stop, **kw):
                nc.tensor.matmul(dst, wh, xh, start=start, stop=False, **kw)
                nc.tensor.matmul(dst, wh, xl, start=False, stop=False, **kw)
                return nc.tensor.matmul(dst, wl, xh, start=False, stop=stop, **kw)

            def tile(dst, n, it, col, ncol, rhs_hi, rhs_lo, k0=0, nk=DM, start=True, stop=True,
                     ready=None, m=P):
                second = (CUT_DOWN if nk == KD else CUT_WIDE)[0] // ncol
                if S_BQ <= n < S_BO:
                    second = 1
                for k in range(nk):
                    if col == 0 and k in (0, second):
                        pe.wait_ge(lo_done, 2 * n + 1 + (k > 0 or second == 1) + 4 * it)
                    if ready:
                        ready(k)
                    c = k * ncol + col
                    last = mm3(dst, w_hi[:, n % 2, c:c + m], w_lo[:, n % 2, c:c + m],
                               rhs_hi(k0 + k), rhs_lo(k0 + k), start and k == 0, stop and k == nk - 1)
                last.then_inc(unit_done, 1)

            def xh(k):
                return xs(xs_hi, k)

            def xl(k):
                return xs(xs_lo, k)

            def x_ready(e):
                return lambda k: pe.wait_ge(xlo_done, DM * e + k + 1)

            def norm_sum(e):
                pe.wait_ge(ss_done, DM * (e + 1))
                nc.tensor.matmul(ps[:, 6, :], ones[:, :], ss[:, :], start=True, stop=True).then_inc(ss_sum, 1)

            pe.wait_ge(tab_in, TAB)
            pe.wait_ge(small_in, 16 * 8)
            nc.tensor.transpose(ps[:, 7, 0:59], par_rows, ident[0:59, 0:59]).then_inc(par_t, 1)
            pe.wait_ge(hot_in, 32)
            nc.tensor.matmul(ps[0:H, 5, :], rel_sb, hot[:, 0:T], start=True, stop=True).then_inc(g_mm, 1)
            nc.tensor.matmul(ps[0:H, 4, 0:GLEN - T], rel_sb, hot[:, T:GLEN], start=True, stop=True).then_inc(g_mm, 1)
            for m in range(DM):
                if m == 0:
                    pe.wait_ge(x_in_s, 16 * NB)
                if m >= 4:
                    pe.wait_ge(x_new, m - 3)
                for t in range(NB):
                    last = nc.tensor.transpose(ps[:, m % 4, t * P:(t + 1) * P],
                                               x_tok[:, t, m * P:(m + 1) * P], ident)
                last.then_inc(x_tr, 1)
            pe.wait_ge(x_new, DM)
            tile(ps[:, 0, :], 0, 0, 0, 256, xh, xl, ready=x_ready(0))
            pe.wait_ge(set_up, 3)
            norm_sum(0)
            tile(ps[:, 1, :], 0, 0, P, 256, xh, xl)
            for u in range(2, 4):
                tile(ps[:, u, :], 1, 0, (u - 2) * P, 256, xh, xl)
            pe.wait_ge(kw_done, 2)
            nc.tensor.matmul(ps[:, 4, :], dup, kw[0:DH, :], start=True, stop=True).then_inc(ki_dup, 1)
            for i in range(1, NB):
                last = nc.tensor.transpose(ps[:, 7, i * JI:(i + 1) * JI], kw[DH:DH + JI, i * P:(i + 1) * P],
                                           ident[DH:DH + JI, DH:DH + JI])
            last.then_inc(w_tr, 1)
            pe.wait_ge(craw_done, 1)
            tile(ps[:, 0, :], 2, 0, 0, 256, xh, xl)
            tile(ps[:, 1, :], 2, 0, P, 256, xh, xl)
            pe.wait_ge(ki_l, 1)
            pe.wait_ge(qi_l, 4)
            for i in range(1, NB):
                for j in range(JI):
                    d = (i - 1) * JI + j
                    if d >= 4:
                        pe.wait_ge(relu_done, d - 3)
                    r = slice(DH * (j % 2), DH * (j % 2) + DH)
                    mm3(ps[:, d % 4, 0:(i + 1) * P], qi_hi[r, j // 2, i * P:(i + 1) * P],
                        qi_lo[r, j // 2, i * P:(i + 1) * P], ki_hi[r, 0:(i + 1) * P],
                        ki_lo[r, 0:(i + 1) * P], True, True).then_inc(dots, 1)
            pe.wait_ge(csq_done, 1)
            nc.tensor.matmul(ps[:, 5, :], ones[:, :], sq[:, 0, :], start=True, stop=True).then_inc(css_sum, 1)
            pe.wait_ge(relu_done, 3 * JI)
            with pe.Fori(0, 4) as i:
                for v in range(4):
                    pe.wait_ge(qa_done, 4 * i + v + 1)
                    tile(ps[:, v, :], S_A2 + v // 2, i, (v % 2) * P, 256, xh, xl)
            pe.wait_ge(cn_done, 1)
            for s in range(NB):
                last = nc.tensor.transpose(ps[:, 7, s * P:(s + 1) * P], c_nrm[:, s * P:(s + 1) * P], ident)
            last.then_inc(c_tr, 1)
            pe.wait_ge(cT_l, 1)
            pe.wait_ge(qa_done, H + 4)
            pe.wait_ge(c_l, 1)

            def step(kk, it=0):
                k, par = kk + 2 * it, kk % 2
                if 2 <= kk < H + 2:
                    h = k - 2
                    pe.wait_ge(nrm_done, h + 1)
                    for s in range(NB):
                        b, c0 = ((3, 0), (4, 0), (5, 0), (5, 2 * P))[s]
                        if s < 3 and kk >= 3:
                            pe.wait_ge(ptl_done, 3 * h - 2 + s)
                        for i in range(s, NB):
                            last = nc.tensor.transpose(ps[:, b, c0 + (i - s) * P:c0 + (i - s + 1) * P],
                                                       prob[:, par, OFF[i] + s * P:OFF[i] + (s + 1) * P], ident)
                        if s != 2:
                            last.then_inc(pt_done, 1)
                if kk < H:
                    pe.wait_ge(ql_done, k + 1)
                    for b, rows in enumerate(((0, 1), (2,), (3,))):
                        if kk >= 1:
                            pe.wait_ge(neg_done, 4 * k - 2 + b)
                        for i in rows:
                            c0 = P if i == 1 else 0
                            n = (i + 1) * P
                            last = mm3(ps[:, b, c0:c0 + n], q_hi[:, par, i * P:(i + 1) * P],
                                       q_lo[:, par, i * P:(i + 1) * P], cT_hi[:, 0:n], cT_lo[:, 0:n],
                                       True, True)
                        last.then_inc(lg_done, 1)
                if 2 <= kk < H + 2:
                    h = k - 2
                    for s in range(NB):
                        if s < 3:
                            pe.wait_ge(ptl_done, 3 * h + s + 1)
                        if s == 0 and kk >= 3:
                            pe.wait_ge(ol_done, h)
                        c0 = (0, 4, 7, 9)[s] * P
                        n = (NB - s) * P
                        last = mm3(ps[:, 6, s * P:T], c_hi[:, s, :], c_lo[:, s, :],
                                   pt_hi[:, par, c0:c0 + n], pt_lo[:, par, c0:c0 + n], s == 0, s == NB - 1)
                    last.then_inc(o_done, 1)
                if 3 <= kk < H + 3:
                    h, p1 = k - 3, 1 - par
                    pe.wait_ge(ol_done, h + 1)
                    pe.wait_ge(uvl_done, h + 1)
                    if p1 == 0 and kk >= 5:
                        pe.wait_ge(oTl_done, (kk - 3) // 2 + it)
                    mm3(ps[:, 7, :], uv_hi[:, p1, :], uv_lo[:, p1, :], o_hi[:, p1, :], o_lo[:, p1, :],
                        p1 == 0, p1 == 1).then_inc(uv_done, 1)

            for kk in range(4):
                step(kk)
            with pe.Fori(0, 5) as i:
                step(4, i)
                step(5, i)
            for kk in range(14, H + 3):
                step(kk)

            def out_proj(s0, e, hi, lo, done):
                pe.wait_ge(done, DM)
                with pe.Fori(0, 2) as i:
                    for v in range(4):
                        pe.wait_ge(x_new, DM * e + v - 1 + 4 * i)
                        tile(ps[:, 4 + v % 2, :], s0 + v // 2, i, (v % 2) * P, 256,
                             lambda k: hi[:, k, :], lambda k: lo[:, k, :])

            def feed_forward(layer, e, s_gu, s_d):
                def ff_tile(j, it=0):
                    for v in range(2):
                        if j >= 2:
                            pe.wait_ge((gate_done, up_done)[v], FT * layer + j - 1 + 2 * it)
                        tile(ps[:, 2 * (j % 2) + v, :], s_gu + j, it, v * P, 256, xh, xl,
                             ready=x_ready(e) if j == 0 and v == 0 else None)

                ff_tile(0)
                norm_sum(e)
                ff_tile(1)
                with pe.Fori(0, (FT - 2) // 2) as i:
                    ff_tile(2, i)
                    ff_tile(3, i)
                pe.wait_ge(al_done, FT * (layer + 1))
                with pe.Fori(0, DM // 2) as i:
                    for v in range(2):
                        pe.wait_ge(x_new, DM * (e + 1) + v - 1 + 2 * i)
                        for c in range(2):
                            tile(ps[:, 4 + v, :], s_d + 2 * v + c, 2 * i, 0, P,
                                 lambda k: act_hi[:, k, :], lambda k: act_lo[:, k, :],
                                 k0=c * KD, nk=KD, start=c == 0, stop=c == 1)

            out_proj(S_AO, 1, oT_hi, oT_lo, oTl_done)
            feed_forward(0, 1, S_F0, S_D0)
            tile(ps[:, 0, :], S_BK, 0, 0, 256, xh, xl, ready=x_ready(2))
            norm_sum(2)
            tile(ps[:, 1, :], S_BK, 0, P, 256, xh, xl)
            for u in range(2):
                tile(ps[:, 2 + u, :], S_BQ, 0, u * P, 256, xh, xl)
            pe.wait_ge(kvb_done, 2)
            for s in range(NB):
                last = nc.tensor.transpose(ps[:, 7, s * P:(s + 1) * P], kv[:, 1, s * P:(s + 1) * P], ident)
            last.then_inc(v_tr, 1)
            for u in range(2, DM):
                pe.wait_ge(bqr_done, max(u - 3, 1))
                tile(ps[:, (2 + u) % 4, :], S_BQ + u // 2, 0, (u % 2) * P, 256, xh, xl)
            pe.wait_ge(bkl_done, 1)
            pe.wait_ge(vl_done, 2)
            pe.wait_ge(bqr_done, DM)

            def b_turn(h2, a, kk):
                par = kk % 2
                for b in range(2):
                    if kk >= 3 or a == 1:
                        pe.wait_ge(bptl_done, 4 * h2 + 2 * a - 1 + b)
                    for s in (2 * b, 2 * b + 1):
                        c0 = (s % 2) * 2 * P
                        own = OFFB[s] + (P if s else 0)
                        last = nc.tensor.transpose(ps[:, 5 + b, c0:c0 + P], b_prob[:, par, a, own:own + P], ident)
                        if s < NB - 1:
                            nxt = OFFB[s + 1]
                            last = nc.tensor.transpose(ps[:, 5 + b, c0 + P:c0 + 2 * P],
                                                       b_prob[:, par, a, nxt:nxt + P], ident)
                    last.then_inc(bpt_done, 1)

            def b_step(kk, it=0):
                k, par = kk + 2 * it, kk % 2
                if 2 <= kk < DM + 2:
                    h2 = k - 2
                    pe.wait_ge(bnrm_done, h2 + 1)
                    b_turn(h2, 0, kk)
                for a in range(2):
                    if a == 1 and 2 <= kk < DM + 2:
                        b_turn(h2, 1, kk)
                    if kk < DM:
                        if a == 0:
                            pe.wait_ge(bql_done, k + 1)
                        r = slice(a * DH, (a + 1) * DH)
                        for b in range(2):
                            if kk >= 1:
                                pe.wait_ge(bneg_done, 8 * (k - 1) + 4 * a + 2 * b + 2)
                            for i in (2 * b, 2 * b + 1):
                                n = P if i == 0 else 2 * P
                                c0 = (0, P, 0, 2 * P)[i]
                                k0 = max(i - 1, 0) * P
                                last = mm3(ps[:, 2 * a + b, c0:c0 + n], bq_hi[r, par, i * P:(i + 1) * P],
                                           bq_lo[r, par, i * P:(i + 1) * P], bk_hi[r, k0:k0 + n],
                                           bk_lo[r, k0:k0 + n], True, True)
                            last.then_inc(blg_done, 1)
                if 2 <= kk < DM + 2:
                    for a in range(2):
                        for s in range(NB):
                            if s % 2 == 0:
                                pe.wait_ge(bptl_done, 4 * h2 + 2 * a + s // 2 + 1)
                            if a == 0 and s == 0 and kk >= 3:
                                pe.wait_ge(bol_done, h2)
                            n = 2 * P if s < NB - 1 else P
                            last = mm3(ps[:, 7, s * P:s * P + n], v_hi[:, a, s, :], v_lo[:, a, s, :],
                                       bpt_hi[:, a, s * 2 * P:s * 2 * P + n], bpt_lo[:, a, s * 2 * P:s * 2 * P + n],
                                       a == 0 and s == 0, a == 1 and s == NB - 1, skip_group_check=True)
                    last.then_inc(bo_done, 1)

            for kk in range(4):
                b_step(kk)
            with pe.Fori(0, 1) as i:
                b_step(4, i)
                b_step(5, i)
            for kk in range(6, DM + 2):
                b_step(kk)
            out_proj(S_BO, 3, bo_hi, bo_lo, bol_done)
            feed_forward(1, 3, S_F1, S_D1)
            norm_sum(4)
            for t in range(NB):
                for g in range(2):
                    b = 2 * (t % 2) + g
                    if t >= 2:
                        pe.wait_ge(ytok_done, 2 * (t - 2) + g + 1)
                    for m in range(4 * g, 4 * g + 4):
                        if t == 0:
                            pe.wait_ge(y_done, m + 1)
                        last = nc.tensor.transpose(ps[:, b, (m % 4) * P:(m % 4 + 1) * P],
                                                   y_t[:, m, t * P:(t + 1) * P], ident)
                    last.then_inc(y_tr, 1)

        @block.scalar
        def _(act):
            def split_hi(n, it=0, after=0):
                for half in range(2):
                    if half == 0:
                        act.wait_ge(raw_full[n % 2], 32 * (n // 2 + 1) + 32 * it)
                        if n >= 2:
                            act.wait_ge(unit_done, after)
                    nc.scalar.copy(pieces(w_hi, n)[half], pieces(raw, n)[half]).then_inc(hi_done, 1)

            def split_after(m, it=0):
                split_hi(m + 2, it, units_through(m) + (1 if is_down(m) else 2) * 2 * it)

            def new_x(e, m, par, gain=None):
                c = DM * e + m
                n0 = held(act, c + 1)
                n1 = held(act, c - 1)
                act.wait_ge(tab_in, TAB)
                act.wait_ge(x_new, n0)
                if e > 0 or m >= 2:
                    act.wait_ge(ss_done, n1)
                nc.scalar.activation(sq[:, par, :], x[:, m, :], ACT.Square).then_inc(sq_done, 1)
                if gain is not None:
                    nc.scalar.activation(xs_hi_m(m), x[:, m, :], ACT.Copy,
                                         scale=params[:, bass.ds(gain + m, 1)]).then_inc(xhi_done, 1)

            def xs_hi_m(m):
                return xs_hi[:, bass.ds(m * T, T)]

            def norm(e):
                act.wait_ge(ss_sum, e + 1)
                nc.scalar.activation(std[:, :], ps[:, 6, :], ACT.Sqrt, bias=eps[:, 0:1], scale=1.0 / D)\
                    .then_inc(std_done, 1)

            for t in range(NB):
                act.dma_start(x_tok[:, t, :], x_in[0, t * P:(t + 1) * P, :]).then_inc(x_in_s, 16)
            act.dma_start(hot, consts[0:BUCKETS, C_HOT:C_END]).then_inc(hot_in, 16)
            act.dma_start(rel_sb, rel_bias).then_inc(hot_in, 16)
            rows = [(par_rows[0:16, :], attn_norm.rearrange("l (k p) -> (l k) p", p=P)),
                    (par_rows[16:32, :], ffn_norm.rearrange("l (k p) -> (l k) p", p=P)),
                    (par_rows[32:40, :], final_norm.rearrange("(k p) -> k p", p=P)),
                    (par_rows[40:48, 0:DH], b_b_in[0, 0:512].rearrange("(k p) -> k p", p=DH)),
                    (par_rows[40:48, DH:P], b_b_in[0, 512:1024].rearrange("(k p) -> k p", p=DH)),
                    (par_rows[48:50, :], b_b_in[0, 1024:1280].rearrange("(k p) -> k p", p=P)),
                    (par_rows[50:58, :], b_b_out[0].rearrange("(k p) -> k p", p=P)),
                    (par_rows[58:59, :], a_latent_norm)]
            for dst, src in rows:
                act.dma_start(dst, src).then_inc(small_in, 16)
            act.wait_ge(set_up, 4)
            split_hi(0)
            split_hi(1)
            act.wait_ge(par_done, 1)
            for m in range(DM):
                new_x(0, m, m % 2, GAIN[0])
            norm(0)
            split_after(0)
            act.wait_ge(ki_dup, 1)
            nc.scalar.copy(ki_hi, ps[:, 4, :]).then_inc(ki_h, 1)
            for u in range(2):
                act.wait_ge(unit_done, u + 3)
                nc.scalar.copy(qi_hi[:, u, :], ps[:, 2 + u, :]).then_inc(qi_h, 1)
            split_after(1)
            for u in range(2):
                act.wait_ge(unit_done, u + 5)
                nc.scalar.copy(qi_hi[:, 2 + u, :], ps[:, u, :]).then_inc(qi_h, 1)
            split_after(2)
            act.wait_ge(craw_done, 1)
            act.wait_ge(ss_done, DM)
            nc.scalar.activation(sq[:, 0, :], c_raw, ACT.Square).then_inc(csq_done, 1)
            for i in range(1, NB):
                for j in range(JI):
                    d = (i - 1) * JI + j
                    act.wait_ge(dots, d + 1)
                    if d >= 4:
                        act.wait_ge(acc_done, d - 3)
                    nc.scalar.activation(relu[:, d % 4, 0:(i + 1) * P], ps[:, d % 4, 0:(i + 1) * P],
                                         ACT.Relu).then_inc(relu_done, 1)
            act.wait_ge(css_sum, 1)
            nc.scalar.activation(std[:, :], ps[:, 5, :], ACT.Sqrt, bias=eps[:, 0:1], scale=1.0 / R)\
                .then_inc(cstd_done, 1)
            nc.scalar.activation(spare[:, :], eps[:, :], ACT.Exp)
            act.wait_ge(cn_done, 1)
            nc.scalar.copy(cT_hi[:, :], c_nrm).then_inc(cT_h, 1)
            with act.Fori(0, 4) as i:
                split_after(S_A2, i)
                split_after(S_A2 + 1, i)
            act.wait_ge(c_tr, 1)
            nc.scalar.copy(c_hi[:, :, :].rearrange("p a b -> p (a b)"), ps[:, 7, :]).then_inc(c_h, 1)

            def q_head(h, par):
                n0 = held(act, 3 * (h - 1))
                act.wait_ge(tab_in, TAB)
                if not (isinstance(h, int) and h < 2):
                    act.wait_ge(lg_done, n0)
                act.wait_ge(qa_done, H + 4)
                nc.scalar.copy(q_hi[:, par, :], q_all[:, h, :]).then_inc(qh_done, 1)

            def uv_head(h, par, it):
                n0 = held(act, 16 * (it + 1))
                n1 = held(act, h - 1)
                act.wait_ge(tab_in, TAB)
                act.wait_ge(uv_full[par], n0)
                if not (isinstance(h, int) and h < 2):
                    act.wait_ge(uv_done, n1)
                nc.scalar.copy(uv_hi[:, par, par * DH:(par + 1) * DH], uv_raw[:, par, :]).then_inc(uvh_done, 1)

            def step(kk, it=0):
                k, par = kk + 2 * it, kk % 2
                if kk + 1 < H:
                    q_head(k + 1, 1 - par)
                if 2 <= kk < H + 2:
                    uv_head(k - 2, par, (kk - 2) // 2 + it)
                if 2 <= kk < H + 2:
                    h = k - 2
                    for b, (c0, n) in enumerate(((0, 4 * P), (4 * P, 3 * P), (7 * P, 3 * P))):
                        act.wait_ge(pt_done, 3 * h + b + 1)
                        nc.scalar.copy(pt_hi[:, par, c0:c0 + n], ps[:, 3 + b, 0:n]).then_inc(pth_done, 1)
                if kk < H:
                    for i in range(NB):
                        n = (i + 1) * P
                        act.wait_ge(neg_done, 4 * k + i + 1)
                        nc.scalar.activation(prob[:, par, OFF[i]:OFF[i] + n], prob[:, par, OFF[i]:OFF[i] + n],
                                             ACT.Exp, bias=low[:, par, i:i + 1], scale=-1.0,
                                             accum_out=rsum[:, par, i:i + 1]).then_inc(exp_done, 1)
                if 2 <= kk < H + 2:
                    act.wait_ge(o_done, k - 1)
                    if kk >= 4:
                        act.wait_ge(uv_done, k - 3)
                    nc.scalar.copy(o_hi[:, par, :], ps[:, 6, :]).then_inc(oh_done, 1)
                if 3 <= kk < H + 3 and par == 0:
                    n0 = held(act, k - 2)
                    act.wait_ge(tab_in, TAB)
                    act.wait_ge(uv_done, n0)
                    nc.scalar.copy(oT_hi[:, (kk - 4) // 2 + it, :], ps[:, 7, :]).then_inc(oTh_done, 1)

            q_head(0, 0)
            for kk in range(4):
                step(kk)
            with act.Fori(0, 5) as i:
                step(4, i)
                step(5, i)
            for kk in range(14, H + 3):
                step(kk)

            def out_proj(s0, e):
                with act.Fori(0, 2) as i:
                    for v in range(2):
                        split_after(s0 + v, i)
                        for u in range(2):
                            new_x(e, 2 * v + u + 4 * i, u, GAIN[e])

            def feed_forward(layer, e, s_gu, s_d):
                norm(e)
                nc.scalar.activation(spare[:, :], eps[:, :], ACT.Silu)

                def ff_tile(j, it=0):
                    split_after(s_gu + j, it)
                    t = FT * layer + j + 2 * it
                    act.wait_ge(gate_done, t + 1)
                    nc.scalar.activation(silu[:, :], gate[:, :], ACT.Silu).then_inc(silu_done, 1)
                    n0 = held(act, t + 1)
                    act.wait_ge(tab_in, TAB)
                    act.wait_ge(glu_done, n0)
                    nc.scalar.copy(act_hi[:, j + 2 * it, :], glu[:, j % 2, :]).then_inc(ah_done, 1)

                with act.Fori(0, (FT - 2) // 2) as i:
                    ff_tile(0, i)
                    ff_tile(1, i)
                ff_tile(FT - 2)
                ff_tile(FT - 1)

                def down_tile(m, it=0):
                    for c in range(2):
                        if s_d + 2 * m + c + 2 < S_END:
                            split_after(s_d + 2 * m + c, 2 * it)
                    new_x(e + 1, m + 2 * it, m % 2, GAIN[e + 1] if e + 1 < 4 else None)

                with act.Fori(0, (DM - 2) // 2) as i:
                    down_tile(0, i)
                    down_tile(1, i)
                down_tile(DM - 2)
                down_tile(DM - 1)

            out_proj(S_AO, 1)
            feed_forward(0, 1, S_F0, S_D0)
            norm(2)
            nc.scalar.activation(spare[:, :], eps[:, :], ACT.Exp)
            split_after(S_BK)
            for a in range(2):
                act.wait_ge(kvr_done, a + 1)
                nc.scalar.activation(kv[:, a, :], bq_raw[:, a, :], ACT.Identity,
                                     bias=params[:, B_IN + 8 + a:B_IN + 9 + a]).then_inc(kvb_done, 1)
            act.wait_ge(kvb_done, 1)
            nc.scalar.copy(bk_hi[:, :], kv[:, 0, :]).then_inc(bkh_done, 1)
            act.wait_ge(v_tr, 1)
            act.wait_ge(pad_done, 2)
            for a in range(2):
                nc.scalar.copy(v_hi[:, a, :, a * DH:(a + 1) * DH],
                               ps[:, 7, :].rearrange("p (s c) -> p s c", s=NB)[:, :, a * DH:(a + 1) * DH])\
                    .then_inc(vh_done, 1)
            act.wait_ge(nqb_done, 1)
            for u in range(DM):
                if u % 2 == 1:
                    split_after(S_BQ + u // 2)
                act.wait_ge(bqr_done, u + 1)
                nc.scalar.activation(bq_all[:, u, :], bq_raw[:, u % 2, :], ACT.Identity,
                                     bias=nq_bias[:, u:u + 1]).then_inc(bqa_done, 1)

            def b_q(j, par):
                n0 = held(act, 4 * (j - 1))
                act.wait_ge(tab_in, TAB)
                if not (isinstance(j, int) and j < 2):
                    act.wait_ge(blg_done, n0)
                act.wait_ge(bqa_done, DM)
                nc.scalar.copy(bq_hi[:, par, :], bq_all[:, j, :]).then_inc(bqh_done, 1)

            def b_step(kk, it=0):
                k, par = kk + 2 * it, kk % 2
                if kk + 1 < DM:
                    b_q(k + 1, 1 - par)
                for a in range(2):
                    if 2 <= kk < DM + 2:
                        h2 = k - 2
                        for b, n in enumerate((4 * P, 3 * P)):
                            act.wait_ge(bpt_done, 4 * h2 + 2 * a + b + 1)
                            if kk >= 3:
                                act.wait_ge(bo_done, h2)
                            nc.scalar.copy(bpt_hi[:, a, b * 4 * P:b * 4 * P + n], ps[:, 5 + b, 0:n])\
                                .then_inc(bpth_done, 1)
                    if kk < DM:
                        for i in range(NB):
                            n = P if i == 0 else 2 * P
                            at = b_prob[:, par, a, OFFB[i]:OFFB[i] + n]
                            act.wait_ge(bneg_done, 8 * k + 4 * a + i + 1)
                            nc.scalar.activation(at, at, ACT.Exp, bias=b_low[:, par, a, i:i + 1], scale=-1.0,
                                                 accum_out=b_rsum[:, par, a, i:i + 1]).then_inc(bexp_done, 1)
                        nc.scalar.activation(b_sinkp[:, par, a, :], b_low[:, par, a, :], ACT.Exp,
                                             bias=sink2[:, par, a:a + 1]).then_inc(bsinkp_done, 1)
                if 2 <= kk < DM + 2:
                    n0 = held(act, k - 1)
                    act.wait_ge(tab_in, TAB)
                    act.wait_ge(bo_done, n0)
                    nc.scalar.copy(bo_hi[:, k - 2, :], ps[:, 7, :]).then_inc(boh_done, 1)

            b_q(0, 0)
            for kk in range(4):
                b_step(kk)
            with act.Fori(0, 1) as i:
                b_step(4, i)
                b_step(5, i)
            for kk in range(6, DM + 2):
                b_step(kk)
            out_proj(S_BO, 3)
            feed_forward(1, 3, S_F1, S_D1)
            norm(4)
            for t in range(NB):
                act.wait_ge(y_tr, 2 * t + 2)
                act.wait_ge(ytok_done, 2 * t + 1)
                nc.scalar.copy(y_tok[:, t, 4 * P:D], ps[:, 2 * (t % 2) + 1, :]).then_inc(ytok_done, 1)

        @block.vector
        def _(dve):
            def lo_part(dst, src, hi, done):
                nc.vector.tensor_tensor(dst, src, hi, ALU.subtract).then_inc(done, 1)

            def new_x(e, m, par, gain=None):
                c = DM * e + m
                dve.wait_ge(sq_done, c + 1)
                if not (isinstance(c, int) and c == 0):
                    dve.wait_ge(ss_done, c)
                nc.vector.tensor_tensor(ss[:, :], ss[:, :], sq[:, par, :], ALU.add).then_inc(ss_done, 1)
                if gain is not None:
                    dve.wait_ge(xhi_done, c + 1)
                    nc.vector.scalar_tensor_tensor(xs_lo[:, bass.ds(m * T, T)], x[:, m, :],
                                                   params[:, bass.ds(gain + m, 1)],
                                                   xs_hi[:, bass.ds(m * T, T)].bitcast(F32),
                                                   ALU.mult, ALU.subtract).then_inc(xlo_done, 1)

            def norm(e):
                dve.wait_ge(std_done, e + 1)
                nc.vector.reciprocal(rstd[:, :], std[:, :]).then_inc(rstd_done, 1)
                nc.vector.memset(ss[:, :], 0.0).then_inc(ss_zero, 1)
                dve.wait_ge(rstd_done, e + 1)
                dve.wait_ge(ss_zero, e + 1)

            nc.vector.memset(rsum[:, :, :], 0.0).then_inc(qa_done, 4)
            nc.vector.memset(top8[:, :, :], 0.0).then_inc(topk, 1)
            dve.wait_ge(par_t, 1)
            nc.vector.tensor_copy(params[:, :], ps[:, 7, 0:59]).then_inc(par_done, 1)
            dve.wait_ge(g_mm, 2)
            nc.vector.tensor_copy(g_sb[:, 0:T], ps[0:H, 5, :]).then_inc(g_done, 1)
            nc.vector.tensor_copy(g_sb[:, T:GLEN], ps[0:H, 4, 0:GLEN - T]).then_inc(g_done, 1)
            dve.wait_ge(par_done, 1)
            dve.wait_ge(set_up, 3)
            for m in range(DM + 1):
                if m < DM:
                    dve.wait_ge(x_tr, m + 1)
                    nc.vector.tensor_copy(x[:, m, :], ps[:, m % 4, :]).then_inc(x_new, 1)
                if m >= 1:
                    new_x(0, m - 1, (m - 1) % 2, GAIN[0])
            norm(0)
            dve.wait_ge(unit_done, 1)
            nc.vector.tensor_tensor(kw[0:DH, :], ps[0:DH, 0, :], rstd[0:DH, :], ALU.mult).then_inc(kw_done, 1)
            nc.vector.tensor_copy(kw[DH:DH + JI, :], ps[DH:DH + JI, 0, :]).then_inc(kw_done, 1)
            dve.wait_ge(unit_done, 2)
            nc.vector.tensor_tensor(c_raw, ps[:, 1, :], rstd[:, :], ALU.mult).then_inc(craw_done, 1)
            dve.wait_ge(ki_h, 1)
            lo_part(ki_lo, ps[:, 4, :], ki_hi.bitcast(F32), ki_l)
            dve.wait_ge(w_tr, 1)
            nc.vector.tensor_copy(w_col[:, :, :].rearrange("p i j -> p (i j)"), ps[:, 7, JI:4 * JI])\
                .then_inc(w_done, 1)
            for u in range(4):
                dve.wait_ge(qi_h, u + 1)
                lo_part(qi_lo[:, u, :], ps[:, (2, 3, 0, 1)[u], :], qi_hi[:, u, :].bitcast(F32), qi_l)
            dve.wait_ge(w_done, 1)
            dve.wait_ge(acc_zero, 3)
            for i in range(1, NB):
                n = (i + 1) * P
                row = work[:, OFF[i] - P:OFF[i] - P + n]
                for j in range(JI):
                    d = (i - 1) * JI + j
                    dve.wait_ge(relu_done, d + 1)
                    if j:
                        dve.wait_ge(acc_done, d)
                    nc.vector.scalar_tensor_tensor(row, relu[:, d % 4, 0:n], w_col[:, i - 1, j:j + 1], row,
                                                   ALU.mult, ALU.add).then_inc(acc_done, 1)
            dve.wait_ge(cstd_done, 1)
            nc.vector.reciprocal(std[:, :], std[:, :]).then_inc(crstd_done, 1)
            dve.wait_ge(crstd_done, 1)
            nc.vector.scalar_tensor_tensor(c_nrm, c_raw, params[:, G_LAT:G_LAT + 1], std[:, :],
                                           ALU.mult, ALU.mult).then_inc(cn_done, 1)
            dve.wait_ge(cT_h, 1)
            lo_part(cT_lo[:, :], c_nrm, cT_hi[:, :].bitcast(F32), cT_l)
            dve.wait_ge(row_out, 16)
            with dve.Fori(0, 4) as it:
                for v in range(4):
                    h = 4 * it + v
                    dve.wait_ge(unit_done, U_A2 + 1 + h)
                    nc.vector.scalar_tensor_tensor(q_all[:, h, :], ps[:, v, :], -float(R) ** -0.5, rstd[:, :],
                                                   ALU.mult, ALU.mult).then_inc(qa_done, 1)
                    for i in range(1, NB):
                        n0 = held(dve, 6 * h + 1)
                        dve.wait_ge(acc_done, 3 * JI)
                        dve.wait_ge(topk, n0)
                        nc.vector.max(top8[:, i - 1, :], work[:, OFF[i] - P:OFF[i] - P + (i + 1) * P])\
                            .then_inc(topk, 1)
                    for i in range(1, NB):
                        row = work[:, OFF[i] - P:OFF[i] - P + (i + 1) * P]
                        n0 = held(dve, 6 * h + 1 + i)
                        dve.wait_ge(acc_done, 3 * JI)
                        dve.wait_ge(topk, n0)
                        nc.vector.match_replace(out=row, in_to_replace=top8[:, i - 1, :], in_values=row,
                                                imm_value=TAKEN).then_inc(topk, 1)
            dve.wait_ge(topk, 6 * TOPK // 8 + 1)
            for i in range(1, NB):
                row = work[:, OFF[i] - P:OFF[i] - P + (i + 1) * P]
                nc.vector.tensor_scalar(row, row, TAKEN / 2, BIG, ALU.is_ge, ALU.mult).then_inc(mask_done, 1)
            dve.wait_ge(c_h, 1)
            lo_part(c_lo[:, :, :].rearrange("p a b -> p (a b)"), ps[:, 7, :],
                    c_hi[:, :, :].rearrange("p a b -> p (a b)").bitcast(F32), c_l)

            def step(kk, it=0):
                k, par = kk + 2 * it, kk % 2
                if 2 <= kk < H + 2:
                    h = k - 2
                    for b, (c0, n) in enumerate(((0, 4 * P), (4 * P, 3 * P), (7 * P, 3 * P))):
                        dve.wait_ge(pth_done, 3 * h + b + 1)
                        lo_part(pt_lo[:, par, c0:c0 + n], ps[:, 3 + b, 0:n],
                                pt_hi[:, par, c0:c0 + n].bitcast(F32), ptl_done)
                if kk < H:
                    for i in range(NB):
                        n = (i + 1) * P
                        b, c0 = ((0, 0), (0, P), (1, 0), (2, 0))[i]
                        n0 = held(dve, 3 * k + b + 1)
                        n1 = held(dve, 4 * k + i + 1)
                        dve.wait_ge(mask_done, 3)
                        dve.wait_ge(lg_done, n0)
                        dve.wait_ge(bias_done, n1)
                        nc.vector.tensor_tensor_reduce(
                            out=prob[:, par, OFF[i]:OFF[i] + n], in0=ps[:, b, c0:c0 + n],
                            in1=bm[:, OFF[i]:OFF[i] + n], scale=1.0, scalar=3e38, op0=ALU.add, op1=ALU.min,
                            accum_out=low[:, par, i:i + 1]).then_inc(neg_done, 1)
                if 1 <= kk < H + 1:
                    h, p1 = k - 1, 1 - par
                    dve.wait_ge(exp_done, 4 * k)
                    nc.vector.reciprocal(rinv[:, p1, :], rsum[:, p1, :]).then_inc(rinv_done, 1)
                    for i in range(NB):
                        n = (i + 1) * P
                        if i == 0:
                            dve.wait_ge(rinv_done, k)
                        at = prob[:, p1, OFF[i]:OFF[i] + n]
                        last = nc.vector.tensor_scalar(at, at, rinv[:, p1, i:i + 1], None, ALU.mult)
                    last.then_inc(nrm_done, 1)
                if 2 <= kk < H + 2:
                    dve.wait_ge(oh_done, k - 1)
                    lo_part(o_lo[:, par, :], ps[:, 6, :], o_hi[:, par, :].bitcast(F32), ol_done)
                if 3 <= kk < H + 3 and par == 0:
                    m = (kk - 4) // 2 + it
                    dve.wait_ge(oTh_done, m + 1)
                    lo_part(oT_lo[:, m, :], ps[:, 7, :], oT_hi[:, m, :].bitcast(F32), oTl_done)

            for kk in range(4):
                step(kk)
            with dve.Fori(0, 5) as i:
                step(4, i)
                step(5, i)
            for kk in range(14, H + 3):
                step(kk)

            def out_proj(u0, e, bias):
                with dve.Fori(0, 2) as i:
                    for v in range(4):
                        m = v + 4 * i
                        dve.wait_ge(unit_done, u0 + 1 + m)
                        if bias is None:
                            nc.vector.tensor_tensor(x[:, m, :], ps[:, 4 + v % 2, :], x[:, m, :], ALU.add)\
                                .then_inc(x_new, 1)
                        else:
                            nc.vector.scalar_tensor_tensor(x[:, m, :], ps[:, 4 + v % 2, :],
                                                           params[:, bass.ds(bias + m, 1)], x[:, m, :],
                                                           ALU.add, ALU.add).then_inc(x_new, 1)
                        new_x(e, m, v % 2, GAIN[e])

            def feed_forward(layer, e, u_gu, u_d):
                norm(e)

                def ff_tile(v, it):
                    t = FT * layer + v + 2 * it
                    b = 2 * v
                    dve.wait_ge(unit_done, u_gu + 2 * v + 1 + 4 * it)
                    if not (layer == 0 and isinstance(t, int) and t == 0):
                        dve.wait_ge(silu_done, t)
                    nc.vector.tensor_tensor(gate[:, :], ps[:, b, :], rstd[:, :], ALU.mult).then_inc(gate_done, 1)
                    dve.wait_ge(unit_done, u_gu + 2 * v + 2 + 4 * it)
                    nc.vector.tensor_tensor(up[:, :], ps[:, b + 1, :], rstd[:, :], ALU.mult).then_inc(up_done, 1)
                    dve.wait_ge(silu_done, t + 1)
                    dve.wait_ge(up_done, t + 1)
                    nc.vector.tensor_tensor(glu[:, v, :], silu[:, :], up[:, :], ALU.mult).then_inc(glu_done, 1)
                    dve.wait_ge(ah_done, t + 1)
                    nc.vector.tensor_tensor(act_lo[:, v + 2 * it, :], glu[:, v, :],
                                            act_hi[:, v + 2 * it, :].bitcast(F32), ALU.subtract)\
                        .then_inc(al_done, 1)

                ff_tile(0, 0)
                ff_tile(1, 0)
                with dve.Fori(1, FT // 2) as i:
                    ff_tile(0, i)
                    ff_tile(1, i)
                with dve.Fori(0, DM // 2) as i:
                    for v in range(2):
                        m = v + 2 * i
                        dve.wait_ge(unit_done, u_d + 2 + 2 * m)
                        nc.vector.tensor_tensor(x[:, m, :], ps[:, 4 + v, :], x[:, m, :], ALU.add)\
                            .then_inc(x_new, 1)
                        new_x(e + 1, m, v, GAIN[e + 1] if e + 1 < 4 else None)

            out_proj(U_AO, 1, None)
            feed_forward(0, 1, U_F0, U_D0)
            norm(2)
            for a in range(2):
                dve.wait_ge(unit_done, U_BK + 1 + a)
                nc.vector.tensor_tensor(bq_raw[:, a, :], ps[:, a, :], rstd[:, :], ALU.mult).then_inc(kvr_done, 1)
            nc.vector.tensor_scalar(nq_bias[:, :], params[:, B_IN:B_IN + DM], -float(DH) ** -0.5, None, ALU.mult)\
                .then_inc(nqb_done, 1)
            dve.wait_ge(sink_in, 16)
            nc.vector.tensor_scalar(nsink[:, :], sink[:, :], -1.0, None, ALU.mult).then_inc(sink_done, 1)
            dve.wait_ge(kvb_done, 2)
            dve.wait_ge(bkh_done, 1)
            lo_part(bk_lo[:, :], kv[:, 0, :], bk_hi[:, :].bitcast(F32), bkl_done)
            dve.wait_ge(vh_done, 2)
            for a in range(2):
                lo_part(v_lo[:, a, :, a * DH:(a + 1) * DH],
                        ps[:, 7, :].rearrange("p (s c) -> p s c", s=NB)[:, :, a * DH:(a + 1) * DH],
                        v_hi[:, a, :, a * DH:(a + 1) * DH].bitcast(F32), vl_done)
            for u in range(DM):
                dve.wait_ge(unit_done, U_BQ + 1 + u)
                if u >= 2:
                    dve.wait_ge(bqa_done, u - 1)
                nc.vector.scalar_tensor_tensor(bq_raw[:, u % 2, :], ps[:, (2 + u) % 4, :], -float(DH) ** -0.5,
                                               rstd[:, :], ALU.mult, ALU.mult).then_inc(bqr_done, 1)

            def b_step(kk, it=0):
                k, par = kk + 2 * it, kk % 2
                if kk < DM:
                    if kk == 0:
                        dve.wait_ge(sink_done, 1)
                    for a in range(2):
                        j = k + a * (H // 2)
                        if kk >= 2:
                            n0 = held(dve, 2 * (k - 1))
                            dve.wait_ge(tab_in, TAB)
                            dve.wait_ge(bsinkp_done, n0)
                        for two, one in ((sink2, sink), (nsink2, nsink)):
                            nc.vector.tensor_copy(two[:, par, a:a + 1], one[:, bass.ds(j, 1)])\
                                .then_inc(bsink2_done, 1)
                for a in range(2):
                    if 2 <= kk < DM + 2:
                        h2 = k - 2
                        for b, n in enumerate((4 * P, 3 * P)):
                            c0 = b * 4 * P
                            dve.wait_ge(bpth_done, 4 * h2 + 2 * a + b + 1)
                            lo_part(bpt_lo[:, a, c0:c0 + n], ps[:, 5 + b, 0:n],
                                    bpt_hi[:, a, c0:c0 + n].bitcast(F32), bptl_done)
                    if kk < DM:
                        for i in range(NB):
                            n = P if i == 0 else 2 * P
                            c0 = (0, P, 0, 2 * P)[i]
                            n0 = held(dve, 4 * k + 2 * a + i // 2 + 1)
                            n1 = held(dve, 2 * k + a + 1)
                            n2 = held(dve, 4 * k + 4)
                            dve.wait_ge(mask_done, 3)
                            dve.wait_ge(blg_done, n0)
                            dve.wait_ge(bbias_done, n1)
                            dve.wait_ge(bsink2_done, n2)
                            nc.vector.tensor_tensor_reduce(
                                out=b_prob[:, par, a, OFFB[i]:OFFB[i] + n], in0=ps[:, 2 * a + i // 2, c0:c0 + n],
                                in1=b_bm[:, par, a, 2 * P - n:2 * P], scale=1.0, scalar=nsink2[:, par, a:a + 1],
                                op0=ALU.add, op1=ALU.min, accum_out=b_low[:, par, a, i:i + 1])\
                                .then_inc(bneg_done, 1)
                if 1 <= kk < DM + 1:
                    p1 = 1 - par
                    dve.wait_ge(bexp_done, 8 * k)
                    dve.wait_ge(bsinkp_done, 2 * k)
                    nc.vector.tensor_tensor(b_rsum[:, p1, :, :], b_rsum[:, p1, :, :], b_sinkp[:, p1, :, :], ALU.add)\
                        .then_inc(brs_done, 1)
                    dve.wait_ge(brs_done, k)
                    nc.vector.reciprocal(b_rinv[:, p1, :, :], b_rsum[:, p1, :, :]).then_inc(brinv_done, 1)
                    for a in range(2):
                        for i in range(NB):
                            n = P if i == 0 else 2 * P
                            if a == 0 and i == 0:
                                dve.wait_ge(brinv_done, k)
                            at = b_prob[:, p1, a, OFFB[i]:OFFB[i] + n]
                            last = nc.vector.tensor_scalar(at, at, b_rinv[:, p1, a, i:i + 1], None, ALU.mult)
                    last.then_inc(bnrm_done, 1)
                if 2 <= kk < DM + 2:
                    dve.wait_ge(boh_done, k - 1)
                    lo_part(bo_lo[:, k - 2, :], ps[:, 7, :], bo_hi[:, k - 2, :].bitcast(F32), bol_done)

            for kk in range(4):
                b_step(kk)
            with dve.Fori(0, 1) as i:
                b_step(4, i)
                b_step(5, i)
            for kk in range(6, DM + 2):
                b_step(kk)
            out_proj(U_BO, 3, B_OUT)
            feed_forward(1, 3, U_F1, U_D1)
            norm(4)
            for m in range(DM):
                nc.vector.scalar_tensor_tensor(y_t[:, m, :], x[:, m, :], params[:, G_FINAL + m:G_FINAL + m + 1],
                                               rstd[:, :], ALU.mult, ALU.mult).then_inc(y_done, 1)
            for t in range(NB):
                dve.wait_ge(y_tr, 2 * t + 1)
                if t:
                    dve.wait_ge(ytok_done, 2 * t)
                nc.vector.tensor_copy(y_tok[:, t, 0:4 * P], ps[:, 2 * (t % 2), :]).then_inc(ytok_done, 1)


_INS = ['x', 'rel_bias', 'attn_norm', 'ffn_norm', 'final_norm', 'a_w_in', 'a_latent_norm', 'a_w_uv',
        'a_w_out', 'b_w_in', 'b_b_in', 'b_sinks', 'b_w_out', 'b_b_out', 'ffn_w_gate_up', 'ffn_w_down']


def kernel(**inputs):
    import concourse.bacc as _bacc
    from concourse.bass_utils import run_bass_kernel_spmd as _run

    nc = _bacc.Bacc("TRN2", target_bir_lowering=False, num_devices=1)
    arrays, args = {}, []
    for name in _INS:
        a = np.ascontiguousarray(inputs[name])
        arrays[f"in_{name}"] = a
        args.append(nc.dram_tensor(f"in_{name}", a.shape, F32, kind="ExternalInput").ap())
    arrays["in_tables"] = tables()
    args.append(nc.dram_tensor("in_tables", (P, C_END), F32, kind="ExternalInput").ap())
    args.append(nc.dram_tensor("bias_row", (H, GLEN), F32, kind="Internal").ap())
    args.append(nc.dram_tensor("bias_toep", (H, P, T), F32, kind="Internal").ap())
    args.append(nc.dram_tensor("out_x", (1, T, D), F32, kind="ExternalOutput").ap())
    trunk(nc, *args)
    r = _run(nc, [arrays], core_ids=[0])
    return r.results[0]["out_x"]
```

```python
from contextlib import ExitStack

import numpy as np

import concourse.bass as bass
from concourse import mybir

F32 = mybir.dt.float32
F32R = mybir.dt.float32r
ALU = mybir.AluOpType
ACT = mybir.ActivationFunctionType

P = 128
D = 1024
T = 512
DM = D // P
NB = T // P
FF = 2816
FT = FF // P
H = 16
R = 128
DH = 64
JI = 8
TOPK = 128
BUCKETS, MAX_DIST = 32, 128
EPS = 1e-6
BIG = 1e30
TAKEN = -3e38

A_CKV, A_QI, A_KI = H * R, H * R + R, H * R + R + JI * DH
OFF = [0, P, 3 * P, 6 * P]
CAUSAL = 10 * P
OFFB = [0, P, 3 * P, 5 * P]
WIN = 7 * P

C_ID, C_DUP, C_CAUSAL, C_WIN, C_HOT = 0, P, 2 * P, 3 * P, 5 * P
GLEN = 640
C_END = C_HOT + GLEN

S_A1, S_A2, S_AO, S_F0, S_D0 = 0, 3, 11, 15, 37
S_BK, S_BQ, S_BO, S_F1, S_D1, S_END = 53, 54, 58, 62, 84, 100
U_A1, U_A2, U_AO, U_F0, U_D0 = 0, 6, 22, 30, 74
U_BK, U_BQ, U_BO, U_F1, U_D1, U_END = 90, 92, 100, 108, 152, 168
SLOT = 2048
KD = FT // 2
CUT_WIDE, CUT_DOWN = (1024, 2048), (768, KD * P)


def units_through(n):
    for s0, u0, per in ((S_D1, U_D1, 1), (S_F1, U_F1, 2), (S_BO, U_BO, 2), (S_BQ, U_BQ, 2),
                        (S_BK, U_BK, 2), (S_D0, U_D0, 1), (0, 0, 2)):
        if n >= s0:
            return u0 + per * (n - s0 + 1)


def held(engine, value):
    if isinstance(value, int):
        return value
    value = engine.snap(value)
    engine.to_reg(value)
    return value


Q_OF_STEP = {0: 3, 1: 4, 3: 5, 4: 6, 5: 7}


def is_down(n):
    return S_D0 <= n < S_BK or n >= S_D1


def tables():
    t = np.zeros((P, C_END), np.float32)
    i = np.arange(P)
    t[:, C_ID:C_ID + P] = np.eye(P)
    t[:DH, C_DUP:C_DUP + P] = (i[None, :] % DH == i[:DH, None])
    t[:, C_CAUSAL:C_CAUSAL + P] = np.where(i[None, :] <= i[:, None], 0, BIG)
    rel = P + i[:, None] - np.arange(2 * P)[None, :]
    t[:, C_WIN:C_WIN + 2 * P] = np.where((rel >= 0) & (rel < P), 0, BIG)
    dist = np.maximum(T - 1 - np.arange(GLEN), 0)
    exact = BUCKETS // 2
    large = exact + (np.log(np.maximum(dist, exact) / exact) / np.log(MAX_DIST / exact)
                     * (BUCKETS - exact) + 1e-9).astype(np.int64)
    bucket = np.where(dist < exact, dist, np.minimum(large, BUCKETS - 1))
    t[:BUCKETS, C_HOT:C_HOT + GLEN] = np.where(bucket[None, :] == np.arange(BUCKETS)[:, None], -1, 0)
    return t


def trunk(nc, x_in, rel_bias, par_in, a_w_in, a_w_uv, a_w_out, b_w_in, b_sinks, b_w_out,
          w_gate_up, w_down, consts, bias_row, bias_toep, out):
    ctx = ExitStack()
    with ctx:
        def sb(name, shape, dt=F32, where=ctx):
            return where.enter_context(nc.sbuf_tensor(name, shape, dt))

        def sem(name):
            return ctx.enter_context(nc.semaphore(name))

        x = sb("x", [P, DM, T])
        ym = ExitStack()
        y_tok = sb("y_tok", [P, NB, D], F32, ym)
        y_t = sb("y_t", [P, 2, T], F32, ym)
        ym.close()
        xs_hi = sb("xs_hi", [P, DM * T], F32R)
        xs_lo = sb("xs_lo", [P, DM * T], F32R)
        raw = sb("raw", [P, 2, SLOT])
        w_hi = sb("w_hi", [P, 2, SLOT], F32R)
        w_lo = sb("w_lo", [P, 2, SLOT], F32R)
        tab = sb("tab", [P, C_HOT])
        params = sb("params", [P, 59])
        ones = sb("ones", [P, P])
        eps = sb("eps", [P, 1])
        spare = sb("spare", [P, 2])
        sq_mem = sb("sq_mem", [P, CAUSAL])
        ss = sb("ss", [P, T])
        std = sb("std", [P, T])
        rstd = sb("rstd", [P, T])

        sq = sq_mem[:, 0:2 * T].rearrange("p (s n) -> p s n", s=2)

        am = ExitStack()
        q_all = sb("q_all", [P, H, T], F32, am)
        q_hi = sb("q_hi", [P, 2, T], F32R, am)
        q_lo = sb("q_lo", [P, 2, T], F32R, am)
        toep = sb("toep", [P, 2, T], F32, am)
        work = sb("work", [P, CAUSAL - P], F32, am)
        top8 = sb("top8", [P, 3, 8], F32, am)
        bm = sq_mem
        cT_hi = sb("cT_hi", [P, T], F32R, am)
        cT_lo = sb("cT_lo", [P, T], F32R, am)
        c_hi = sb("c_hi", [P, NB, R], F32R, am)
        c_lo = sb("c_lo", [P, NB, R], F32R, am)
        early = ExitStack()
        sq_first = sb("sq_first", [P, DM, T], F32, early)
        early.close()
        oT_hi = sb("oT_hi", [P, DM, T], F32R, am)
        oT_lo = sb("oT_lo", [P, DM, T], F32R, am)
        uv_raw = sb("uv_raw", [P, 2, DH], F32, am)
        uv_hi = sb("uv_hi", [P, 2, P], F32R, am)
        uv_lo = sb("uv_lo", [P, 2, P], F32R, am)
        w_col = sb("w_col", [P, 3, JI], F32, am)
        prob0 = sb("prob0", [P, CAUSAL], F32, am)
        low = sb("low", [P, 2, NB], F32, am)
        rsum = sb("rsum", [P, 2, NB], F32, am)
        rinv = sb("rinv", [P, 2, NB], F32, am)
        am.close()
        x_tok = q_all[:, 0:DM, :].rearrange("p a b -> p (a b)").rearrange("p (t n) -> p t n", t=NB)
        hot = q_all[0:BUCKETS, 8:10, :].rearrange("p a b -> p (a b)")[:, 0:GLEN]
        rel_sb = q_all[0:BUCKETS, 10, 0:H]
        g_sb = q_all[0:H, 11:13, :].rearrange("p a b -> p (a b)")[:, 0:GLEN]
        par_rows = q_all[0:59, 13, 0:P]
        qi_hi, qi_lo = oT_hi[:, 0:4, :], oT_lo[:, 0:4, :]
        ki_hi, ki_lo = oT_hi[:, 4, :], oT_lo[:, 4, :]
        kw = prob0[:, 0:T]
        c_raw = prob0[:, T:2 * T]
        prob = (prob0[:, :], raw[:, 1, 0:CAUSAL])
        c_nrm = sq[:, 1, :]
        relu = q_all[:, 12:16, :]
        pt_hi = xs_hi[:, 0:2 * CAUSAL].rearrange("p (s n) -> p s n", s=2)
        pt_lo = xs_lo[:, 0:2 * CAUSAL].rearrange("p (s n) -> p s n", s=2)
        o_hi = xs_hi[:, 2 * CAUSAL:2 * CAUSAL + 2 * T].rearrange("p (s n) -> p s n", s=2)
        o_lo = xs_lo[:, 2 * CAUSAL:2 * CAUSAL + 2 * T].rearrange("p (s n) -> p s n", s=2)

        bmem = ExitStack()
        bq_raw = sb("bq_raw", [P, 2, T], F32, bmem)
        bq_hi = sb("bq_hi", [P, 2, T], F32R, bmem)
        bq_lo = sb("bq_lo", [P, 2, T], F32R, bmem)
        kv = sb("kv", [P, 2, T], F32, bmem)
        bk_hi = sb("bk_hi", [P, T], F32R, bmem)
        bk_lo = sb("bk_lo", [P, T], F32R, bmem)
        v_hi = sb("v_hi", [P, 2, NB, P], F32R, bmem)
        v_lo = sb("v_lo", [P, 2, NB, P], F32R, bmem)
        b_toep = sb("b_toep", [P, 2, 2, 2 * P], F32, bmem)
        b_bm = sb("b_bm", [P, 2, 2, 2 * P], F32, bmem)
        b_prob = sb("b_prob", [P, 2, 2, WIN], F32, bmem)
        bo_hi = sb("bo_hi", [P, DM, T], F32R, bmem)
        bo_lo = sb("bo_lo", [P, DM, T], F32R, bmem)
        sink = sb("sink", [P, H], F32, bmem)
        nsink = sb("nsink", [P, H], F32, bmem)
        nq_bias = sb("nq_bias", [P, DM], F32, bmem)
        sink2 = sb("sink2", [P, 2, 2], F32, bmem)
        nsink2 = sb("nsink2", [P, 2, 2], F32, bmem)
        b_low = sb("b_low", [P, 2, 2, NB], F32, bmem)
        b_rsum = sb("b_rsum", [P, 2, 2, NB], F32, bmem)
        b_sinkp = sb("b_sinkp", [P, 2, 2, NB], F32, bmem)
        b_rinv = sb("b_rinv", [P, 2, 2, NB], F32, bmem)
        bpt_hi = sb("bpt_hi", [P, 2, WIN], F32R, bmem)
        bpt_lo = sb("bpt_lo", [P, 2, WIN], F32R, bmem)
        bmem.close()

        fm = ExitStack()
        act_hi = sb("act_hi", [P, FT, T], F32R, fm)
        act_lo = sb("act_lo", [P, FT, T], F32R, fm)
        gate = sb("gate", [P, T], F32, fm)
        up = sb("up", [P, T], F32, fm)
        glu = sb("glu", [P, 2, T], F32, fm)
        fm.close()
        silu = std

        ps = ctx.enter_context(nc.psum_tensor("ps", [P, 8, T], F32))

        ident = tab[:, C_ID:C_ID + P]
        dup = tab[0:DH, C_DUP:C_DUP + P]
        causal = tab[:, C_CAUSAL:C_CAUSAL + P]
        window = tab[:, C_WIN:C_WIN + 2 * P]
        G_ATTN, G_FFN, G_FINAL, B_IN, B_OUT, G_LAT = (0, 8), (16, 24), 32, 40, 50, 58
        GAIN = [G_ATTN[0], G_FFN[0], G_ATTN[1], G_FFN[1]]

        raw_full = [sem("raw_full0"), sem("raw_full1")]
        hi_done, lo_done = sem("hi_done"), sem("lo_done")
        unit_done = sem("unit_done")
        tab_in, x_in_s, small_in, sink_in = sem("tab_in"), sem("x_in"), sem("small_in"), sem("sink_in")
        hot_in = sem("hot_in")
        set_up = sem("set_up")
        x_tr = sem("x_tr")
        x_new = sem("x_new")
        sq_done = sem("sq_done")
        ss_done = sem("ss_done")
        xhi_done, xlo_done = sem("xhi_done"), sem("xlo_done")
        ss_zero = sem("ss_zero")
        ss_sum = sem("ss_sum")
        std_done, rstd_done = sem("std_done"), sem("rstd_done")
        par_t, par_done = sem("par_t"), sem("par_done")
        g_mm, g_done, row_out, toep_out = sem("g_mm"), sem("g_done"), sem("row_out"), sem("toep_out")
        kw_done, ki_dup, ki_h, ki_l, w_tr, w_done = (sem(n) for n in
                                                     ("kw_done", "ki_dup", "ki_h", "ki_l", "w_tr", "w_done"))
        qi_h, qi_l = sem("qi_h"), sem("qi_l")
        dots, relu_done, acc_done, acc_zero = sem("dots"), sem("relu_done"), sem("acc_done"), sem("acc_zero")
        craw_done, csq_done, css_sum, cstd_done, crstd_done, cn_done = (
            sem(n) for n in ("craw_done", "csq_done", "css_sum", "cstd_done", "crstd_done", "cn_done"))
        cT_h, cT_l, c_tr, c_h, c_l = (sem(n) for n in ("cT_h", "cT_l", "c_tr", "c_h", "c_l"))
        qa_done = sem("qa_done")
        topk = sem("topk")
        mask_done = sem("mask_done")
        toep_full = [sem("toep_full0"), sem("toep_full1")]
        uv_full = [sem("uv_full0"), sem("uv_full1")]
        qh_done, ql_done = sem("qh_done"), sem("ql_done")
        bias_done = sem("bias_done")
        lg_done = sem("lg_done")
        neg_done = sem("neg_done")
        exp_done = sem("exp_done")
        rinv_done, nrm_done = sem("rinv_done"), sem("nrm_done")
        pt_done, pth_done, ptl_done = sem("pt_done"), sem("pth_done"), sem("ptl_done")
        o_done, oh_done, ol_done = sem("o_done"), sem("oh_done"), sem("ol_done")
        uvh_done, uvl_done, uv_done = sem("uvh_done"), sem("uvl_done"), sem("uv_done")
        oTh_done, oTl_done = sem("oTh_done"), sem("oTl_done")
        gate_done, up_done, silu_done, glu_done, ah_done, al_done = (
            sem(n) for n in ("gate_done", "up_done", "silu_done", "glu_done", "ah_done", "al_done"))
        kvr_done, kvb_done, bkh_done, bkl_done, v_tr, vh_done, vl_done, pad_done = (
            sem(n) for n in ("kvr_done", "kvb_done", "bkh_done", "bkl_done", "v_tr", "vh_done", "vl_done", "pad_done"))
        sink_done, nqb_done, bqr_done, bqa_done = sem("sink_done"), sem("nqb_done"), sem("bqr_done"), sem("bqa_done")
        btoep_full = [sem("btoep_full0"), sem("btoep_full1")]
        bqh_done, bql_done, bbias_done, blg_done, bneg_done = (
            sem(n) for n in ("bqh_done", "bql_done", "bbias_done", "blg_done", "bneg_done"))
        bsinkp_done, bsink2_done, brs_done, brinv_done, bnrm_done = (
            sem(n) for n in ("bsinkp_done", "bsink2_done", "brs_done", "brinv_done", "bnrm_done"))
        bpt_done, bpth_done, bptl_done, bo_done, boh_done, bol_done = (
            sem(n) for n in ("bpt_done", "bpth_done", "bptl_done", "bo_done", "boh_done", "bol_done"))
        y_done, y_tr, y_copied, out_done = sem("y_done"), sem("y_tr"), sem("y_copied"), sem("out_done")
        y_out = [sem("y_out_dve"), sem("y_out_act")]
        TAB = 16

        def pieces(buf, n):
            if S_BQ <= n < S_BO:
                if buf is raw:
                    v = buf[:, n % 2, :].rearrange("p (k a j c) -> p a k j c", k=DM, a=2, j=2)
                else:
                    v = buf[:, n % 2, :].rearrange("p (k j a c) -> p a k j c", k=DM, a=2, j=2)
                return [v[:, a, :, :, :] for a in range(2)]
            cut = CUT_DOWN if is_down(n) else CUT_WIDE
            return [buf[:, n % 2, 0:cut[0]], buf[:, n % 2, cut[0]:cut[1]]]

        block = ctx.enter_context(nc.Block())

        @block.sync
        def _(sp):
            def slab(n, it, src):
                for dst, s in src(n % 2):
                    if n >= 2:
                        sp.wait_ge(lo_done, 2 * (n - 1) + 4 * it)
                    sp.dma_start(dst, s).then_inc(raw_full[n % 2], 16)

            def wide(w, c0):
                def src(slot):
                    v = raw[:, slot, :].rearrange("p (k n) -> p k n", k=DM)
                    g = w.rearrange("(k p) n -> p k n", p=P)
                    return [(v[:, 4 * i:4 * i + 4, :], g[:, 4 * i:4 * i + 4, bass.ds(c0, 256)])
                            for i in range(2)]
                return src

            def two_halves(w, c0, c1):
                def src(slot):
                    v = raw[:, slot, :].rearrange("p (k n) -> p k n", k=DM)
                    g = w.rearrange("(k p) n -> p k n", p=P)
                    return [(v[:, :, 0:P], g[:, :, bass.ds(c0, P)]),
                            (v[:, :, P:2 * P], g[:, :, bass.ds(c1, P)])]
                return src

            def down(w, c, m):
                def src(slot):
                    v = raw[:, slot, 0:KD * P].rearrange("p (k n) -> p k n", k=KD)
                    g = w.rearrange("(k p) n -> p k n", p=P)
                    return [(v[:, a:b, :], g[:, c * KD + a:c * KD + b, bass.ds(m * P, P)])
                            for a, b in ((0, 6), (6, KD))]
                return src

            def feed_forward(layer, s_gu, s_d):
                w = w_gate_up[layer]
                with sp.Fori(0, FT // 2) as i:
                    for v in range(2):
                        slab(s_gu + v, i, two_halves(w, (2 * i + v) * P, (2 * i + v) * P + FF))
                with sp.Fori(0, DM) as m:
                    for c in range(2):
                        slab(s_d + c, m, down(w_down[layer], c, m))

            for t in (0, 2):
                sp.dma_start(x_tok[:, t, :], x_in[0, t * P:(t + 1) * P, :]).then_inc(x_in_s, 16)
            sp.dma_start(tab[:, :], consts[:, 0:C_HOT]).then_inc(tab_in, 16)
            r0 = raw[:, 0, :].rearrange("p (k n) -> p k n", k=DM)
            aw = a_w_in[0].rearrange("(k p) n -> p k n", p=P)
            sp.dma_start(r0[:, :, 0:DH + JI], aw[:, :, A_KI:A_KI + DH + JI]).then_inc(raw_full[0], 16)
            sp.dma_start(r0[:, :, P:2 * P], aw[:, :, A_CKV:A_CKV + R]).then_inc(raw_full[0], 16)
            slab(1, 0, wide(a_w_in[0], A_QI))
            sp.wait_ge(g_done, 2)
            sp.dma_start(bias_row, g_sb).then_inc(row_out, 16)
            slab(2, 0, wide(a_w_in[0], A_QI + 256))
            sp.wait_ge(row_out, 16)
            skew = bass.AP(tensor=bias_row.tensor, offset=P - 1, ap=[[GLEN, H], [-1, P], [1, T]])
            sp.dma_start(bias_toep, skew).then_inc(toep_out, 16)
            with sp.Fori(0, 4) as i:
                for v in range(2):
                    slab(S_A2 + v, i, wide(a_w_in[0], (2 * i + v) * 256))
            sp.wait_ge(toep_out, 16)

            def toep_in(h, par, first=False):
                if not first:
                    sp.wait_ge(bias_done, 4 * (h - 1))
                sp.dma_start(toep[:, par, :], bias_toep[h]).then_inc(toep_full[par], 16)

            def uv_in(h, par, first=False):
                if not first:
                    sp.wait_ge(uvl_done, h - 1)
                sp.dma_start(uv_raw[:, par, :], a_w_uv[0, h]).then_inc(uv_full[par], 16)

            for h in range(2):
                toep_in(h, h, True)
                uv_in(h, h, True)
            for n in range(S_AO, S_AO + 2):
                slab(n, 0, wide(a_w_out[0], (n - S_AO) * 256))
            toep_in(2, 0)
            toep_in(3, 1)
            with sp.Fori(2, H // 2) as i:
                for v in range(2):
                    toep_in(2 * i + v, v)
                    uv_in(2 * i + v - 2, v)
            uv_in(H - 2, 0)
            uv_in(H - 1, 1)
            sp.wait_ge(ptl_done, 3 * H)
            for n in range(S_AO + 2, S_F0):
                slab(n, 0, wide(a_w_out[0], (n - S_AO) * 256))
            feed_forward(0, S_F0, S_D0)
            slab(S_BK, 0, wide(b_w_in[0], H * DH))
            sp.wait_ge(unit_done, U_BK)
            sp.dma_start(sink[:, :], b_sinks[0:1, :].broadcast_to([P, H])).then_inc(sink_in, 16)

            for n in range(S_BQ, S_BO):
                c0 = (n - S_BQ) * 2 * DH
                slab(n, 0, two_halves(b_w_in[0], c0, c0 + H // 2 * DH))

            def pair_in(j):
                par = j % 2
                for a in range(2):
                    if j >= 2:
                        sp.wait_ge(bbias_done, 2 * (j - 1))
                    sp.dma_start(b_toep[:, par, a, :], bias_toep[j + a * (H // 2), :, T - 2 * P:T])\
                        .then_inc(btoep_full[par], 16)

            def bo_slab(n):
                v = raw[:, n % 2, :].rearrange("p (k n) -> p k n", k=DM)
                c0 = (n - S_BO) * 256
                for a in range(2):
                    sp.wait_ge(lo_done, 2 * (n - 1))
                    sp.dma_start(v[a * DH:(a + 1) * DH, :, :],
                                 b_w_out[0, a * 512:(a + 1) * 512, c0:c0 + 256]
                                 .rearrange("(k p) n -> p k n", p=DH)).then_inc(raw_full[n % 2], 16)

            pair_in(0)
            pair_in(1)
            bo_slab(S_BO)
            pair_in(2)
            pair_in(3)
            pair_in(4)
            bo_slab(S_BO + 1)
            pair_in(5)
            pair_in(6)
            pair_in(7)
            bo_slab(S_BO + 2)
            bo_slab(S_BO + 3)
            feed_forward(1, S_F1, S_D1)
            for t in range(NB):
                sp.wait_ge(y_out[t % 2], t // 2 + 1)
                sp.dma_start(out[0, t * P:(t + 1) * P, :], y_tok[:, t, :]).then_inc(out_done, 16)
            sp.wait_ge(out_done, 16 * NB)

        @block.gpsimd
        def _(pool):
            def split_lo(n, it=0):
                for half in range(2):
                    pool.wait_ge(hi_done, 2 * n + half + 1 + 4 * it)
                    nc.gpsimd.tensor_tensor(pieces(w_lo, n)[half], pieces(raw, n)[half],
                                            pieces(w_hi, n)[half].bitcast(F32), ALU.subtract)\
                        .then_inc(lo_done, 1)

            nc.gpsimd.memset(ones[:, :], 1.0).then_inc(set_up, 1)
            nc.gpsimd.memset(eps[:, :], EPS).then_inc(set_up, 1)
            nc.gpsimd.memset(ss[:, :], 0.0).then_inc(set_up, 1)
            nc.gpsimd.memset(raw[:, 0, :].rearrange("p (k n) -> p k n", k=DM)[:, :, DH + JI:P], 0.0)\
                .then_inc(set_up, 1)
            nc.gpsimd.memset(work[:, :], 0.0).then_inc(set_up, 1)
            nc.gpsimd.memset(uv_hi[:, :, :].bitcast(F32), 0.0).then_inc(set_up, 1)
            nc.gpsimd.memset(uv_lo[:, :, :].bitcast(F32), 0.0).then_inc(set_up, 1)
            pool.wait_ge(tab_in, TAB)
            pool.wait_ge(set_up, 5)
            for i in range(1, NB):
                d = OFF[i] - P + i * P
                nc.gpsimd.tensor_tensor(work[:, d:d + P], work[:, d:d + P], causal, ALU.subtract)\
                    .then_inc(acc_zero, 1)
            for n in range(S_A2 + 2):
                split_lo(n)

            def q_part(h, par):
                n0 = held(pool, h + 1)
                pool.wait_ge(tab_in, TAB)
                pool.wait_ge(qh_done, n0)
                nc.gpsimd.tensor_tensor(q_lo[:, par, :], q_all[:, h, :],
                                        q_hi[:, par, :].bitcast(F32), ALU.subtract).then_inc(ql_done, 1)

            split_lo(S_A2 + 2)
            split_lo(S_A2 + 3)
            q_part(0, 0)
            q_part(1, 1)
            with pool.Fori(0, 2) as i:
                for v in range(2):
                    split_lo(S_A2 + 4 + v, i)
            split_lo(S_AO)

            def head(hh, it=0):
                h, par = hh + 2 * it, hh % 2
                if 2 <= hh < H:
                    q_part(h, par)
                if hh < H:
                    for i in range(NB):
                        n = (i + 1) * P
                        mask = causal if i == 0 else work[:, OFF[i] - P:OFF[i] - P + n]
                        if i == 0:
                            if hh == 0:
                                pool.wait_ge(c_tr, 1)
                            n0 = held(pool, 16 * (hh // 2 + 1 + it))
                            pool.wait_ge(tab_in, TAB)
                            pool.wait_ge(toep_full[par], n0)
                        if hh == 0 and i > 0:
                            pool.wait_ge(mask_done, i)
                        if hh > 0:
                            pool.wait_ge(neg_done, 4 * h - 3 + i)
                        nc.gpsimd.tensor_tensor(bm[:, OFF[i]:OFF[i] + n], toep[:, par, T - n:T], mask, ALU.add)\
                            .then_inc(bias_done, 1)
                if hh >= 3:
                    c0, p1 = (1 - par) * DH, 1 - par
                    pool.wait_ge(uvh_done, h - 2)
                    nc.gpsimd.tensor_tensor(uv_lo[:, p1, c0:c0 + DH], uv_raw[:, p1, :],
                                            uv_hi[:, p1, c0:c0 + DH].bitcast(F32), ALU.subtract)\
                        .then_inc(uvl_done, 1)

            for hh in range(4):
                head(hh)
            with pool.Fori(0, (H - 4) // 2) as i:
                head(4, i)
                head(5, i)
            for hh in range(H, H + 3):
                head(hh)
            for n in range(S_AO + 1, S_F0 + 2):
                split_lo(n)

            def feed_forward(s_gu, s_d):
                with pool.Fori(0, (FT - 2) // 2) as i:
                    for v in range(2):
                        split_lo(s_gu + 2 + v, i)
                split_lo(s_d)
                split_lo(s_d + 1)
                with pool.Fori(0, (2 * DM - 2) // 2) as i:
                    for v in range(2):
                        split_lo(s_d + 2 + v, i)

            feed_forward(S_F0, S_D0)
            split_lo(S_BK)
            split_lo(S_BK + 1)
            pool.wait_ge(unit_done, U_BK)
            nc.gpsimd.memset(v_hi[:, :, :, :].bitcast(F32), 0.0).then_inc(pad_done, 1)
            nc.gpsimd.memset(v_lo[:, :, :, :].bitcast(F32), 0.0).then_inc(pad_done, 1)
            split_lo(S_BQ + 1)
            for j in range(DM):
                par = j % 2
                pool.wait_ge(bqh_done, j + 1)
                nc.gpsimd.tensor_tensor(bq_lo[:, par, :], bq_raw[:, par, :],
                                        bq_hi[:, par, :].bitcast(F32), ALU.subtract).then_inc(bql_done, 1)
                for a in range(2):
                    if j >= 2:
                        pool.wait_ge(bneg_done, 8 * (j - 1))
                    pool.wait_ge(btoep_full[par], 32 * (j // 2 + 1))
                    nc.gpsimd.tensor_tensor(b_bm[:, par, a, :], b_toep[:, par, a, :], window, ALU.add)\
                        .then_inc(bbias_done, 1)
                if j in (0, 2, 5, 7):
                    split_lo(S_BQ + 2 + j // 2)
            for n in range(S_BO + 2, S_F1 + 2):
                split_lo(n)
            feed_forward(S_F1, S_D1)

        @block.tensor
        def _(pe):
            def mm3(dst, wh, wl, xh, xl, start, stop, **kw):
                nc.tensor.matmul(dst, wh, xh, start=start, stop=False, **kw)
                nc.tensor.matmul(dst, wh, xl, start=False, stop=False, **kw)
                return nc.tensor.matmul(dst, wl, xh, start=False, stop=stop, **kw)

            def tile(dst, n, it, col, ncol, rhs_hi, rhs_lo, k0=0, nk=DM, start=True, stop=True):
                second = 0 if S_BQ <= n < S_BO else (CUT_DOWN if nk == KD else CUT_WIDE)[0] // ncol
                for k in range(nk):
                    if col == 0 and k in (0, second):
                        pe.wait_ge(lo_done, 2 * n + 1 + (k >= second) + 4 * it)
                    c = k * ncol + col
                    last = mm3(dst, w_hi[:, n % 2, c:c + P], w_lo[:, n % 2, c:c + P],
                               rhs_hi(k0 + k), rhs_lo(k0 + k), start and k == 0, stop and k == nk - 1)
                last.then_inc(unit_done, 1)

            def first_tiles(dst, n, e):
                for k in range(DM):
                    if k in (0, CUT_WIDE[0] // 256):
                        pe.wait_ge(lo_done, 2 * n + 1 + (k > 0))
                    pe.wait_ge(xlo_done, DM * e + k + 1)
                    for u in range(2):
                        c = k * 256 + u * P
                        last = mm3(dst[u], w_hi[:, n % 2, c:c + P], w_lo[:, n % 2, c:c + P],
                                   xh(k), xl(k), k == 0, k == DM - 1)
                        if k == DM - 1:
                            last.then_inc(unit_done, 1)

            def xh(k):
                return xs_hi[:, k * T:(k + 1) * T]

            def xl(k):
                return xs_lo[:, k * T:(k + 1) * T]

            def norm_sum(e):
                pe.wait_ge(ss_done, DM * (e + 1))
                nc.tensor.matmul(ps[:, 6, :], ones[:, :], ss[:, :], start=True, stop=True).then_inc(ss_sum, 1)

            pe.wait_ge(tab_in, TAB)
            pe.wait_ge(small_in, 16)
            nc.tensor.transpose(ps[:, 7, 0:59], par_rows, ident[0:59, 0:59]).then_inc(par_t, 1)
            for m in range(DM):
                if m == 0:
                    pe.wait_ge(x_in_s, 16 * NB)
                if m >= 4:
                    pe.wait_ge(x_new, m - 3)
                for t in range(NB):
                    last = nc.tensor.transpose(ps[:, m % 4, t * P:(t + 1) * P],
                                               x_tok[:, t, m * P:(m + 1) * P], ident)
                last.then_inc(x_tr, 1)
            pe.wait_ge(hot_in, 32)
            nc.tensor.matmul(ps[0:H, 5, :], rel_sb, hot[:, 0:T], start=True, stop=True).then_inc(g_mm, 1)
            nc.tensor.matmul(ps[0:H, 4, 0:GLEN - T], rel_sb, hot[:, T:GLEN], start=True, stop=True).then_inc(g_mm, 1)
            pe.wait_ge(x_new, 6)
            first_tiles((ps[:, 0, :], ps[:, 1, :]), 0, 0)
            pe.wait_ge(set_up, 3)
            norm_sum(0)
            tile(ps[:, 2, :], 1, 0, 0, 256, xh, xl)
            tile(ps[:, 3, :], 1, 0, P, 256, xh, xl)
            pe.wait_ge(kw_done, 2)
            nc.tensor.matmul(ps[:, 4, :], dup, kw[0:DH, :], start=True, stop=True).then_inc(ki_dup, 1)
            for i in range(1, NB):
                last = nc.tensor.transpose(ps[:, 7, i * JI:(i + 1) * JI], kw[DH:DH + JI, i * P:(i + 1) * P],
                                           ident[DH:DH + JI, DH:DH + JI])
            last.then_inc(w_tr, 1)
            pe.wait_ge(craw_done, 1)
            tile(ps[:, 0, :], 2, 0, 0, 256, xh, xl)
            tile(ps[:, 1, :], 2, 0, P, 256, xh, xl)
            pe.wait_ge(ki_l, 1)
            for i in range(1, NB):
                h = i - 1
                n = S_A2 + h // 2
                pe.wait_ge(qa_done, h + 1)
                pe.wait_ge(lo_done, 2 * n + 2)
                for j in range(JI):
                    d = h * JI + j
                    if d >= 4:
                        pe.wait_ge(relu_done, d - 3)
                    if d < 4:
                        pe.wait_ge(qi_l, d + 1)
                    r = slice(DH * (j % 2), DH * (j % 2) + DH)
                    mm3(ps[:, (d + 2) % 4, 0:(i + 1) * P], qi_hi[r, j // 2, i * P:(i + 1) * P],
                        qi_lo[r, j // 2, i * P:(i + 1) * P], ki_hi[r, 0:(i + 1) * P],
                        ki_lo[r, 0:(i + 1) * P], True, True).then_inc(dots, 1)
                    c = j * 256 + (h % 2) * P
                    last = mm3(ps[:, 4 + h % 2, :], w_hi[:, n % 2, c:c + P], w_lo[:, n % 2, c:c + P],
                               xh(j), xl(j), j == 0, j == DM - 1)
                last.then_inc(unit_done, 1)
            pe.wait_ge(csq_done, 1)
            nc.tensor.matmul(ps[:, 6, :], ones[:, :], sq[:, 0, :], start=True, stop=True).then_inc(css_sum, 1)
            pe.wait_ge(relu_done, 3 * JI)
            pe.wait_ge(qa_done, 4)
            tile(ps[:, 3, :], S_A2 + 1, 0, P, 256, xh, xl)
            pe.wait_ge(cn_done, 1)
            for s in range(NB):
                last = nc.tensor.transpose(ps[:, 7, s * P:(s + 1) * P], c_nrm[:, s * P:(s + 1) * P], ident)
            last.then_inc(c_tr, 1)

            def q_tile(v, i):
                pe.wait_ge(qa_done, 4 * i + v + 3)
                tile(ps[:, v, :], S_A2 + 2 + v // 2, i, (v % 2) * P, 256, xh, xl)

            with pe.Fori(0, 2) as i:
                for v in range(4):
                    q_tile(v, i)
            for v in range(3):
                q_tile(v, 2)
            pe.wait_ge(cT_l, 1)
            pe.wait_ge(qa_done, H + 1)

            def out_first(s0, hi, lo, done, ks):
                for k in ks:
                    pe.wait_ge(done, k + 1)
                    pe.wait_ge(lo_done, 2 * s0 + 2)
                    for u in range(2):
                        c = k * 256 + u * P
                        last = mm3(ps[:, u, :], w_hi[:, s0 % 2, c:c + P], w_lo[:, s0 % 2, c:c + P],
                                   hi[:, k, :], lo[:, k, :], k == 0, k == DM - 1)
                        if k == DM - 1:
                            last.then_inc(unit_done, 1)

            def out_rest(s0, e, hi, lo):
                for m in range(2, DM):
                    if m >= 4:
                        pe.wait_ge(x_new, DM * e + m - 3)
                    tile(ps[:, m % 4, :], s0 + m // 2, 0, (m % 2) * P, 256,
                         lambda k: hi[:, k, :], lambda k: lo[:, k, :])

            def step(kk, it=0):
                k, par = kk + 2 * it, kk % 2
                if 2 <= kk < H + 2:
                    h = k - 2
                    for s in (2, 3, 1, 0):
                        b, c0 = ((3, 0), (4, 0), (5, 0), (5, 2 * P))[s]
                        if s < 3:
                            pe.wait_ge(nrm_done, 4 * h + 4 - s)
                        if s < 3 and kk >= 3:
                            pe.wait_ge(ptl_done, 3 * h - s)
                        for i in range(s, NB):
                            last = nc.tensor.transpose(ps[:, b, c0 + (i - s) * P:c0 + (i - s + 1) * P],
                                                       prob[par][:, OFF[i] + s * P:OFF[i] + (s + 1) * P], ident)
                        if s != 2:
                            last.then_inc(pt_done, 1)
                if kk < H:
                    pe.wait_ge(ql_done, k + 1)
                    for b, rows in enumerate(((0, 1), (2,), (3,))):
                        if kk >= 1:
                            pe.wait_ge(neg_done, 4 * k - 2 + b)
                        for i in rows:
                            c0 = P if i == 1 else 0
                            n = (i + 1) * P
                            last = mm3(ps[:, b, c0:c0 + n], q_hi[:, par, i * P:(i + 1) * P],
                                       q_lo[:, par, i * P:(i + 1) * P], cT_hi[:, 0:n], cT_lo[:, 0:n],
                                       True, True)
                        last.then_inc(lg_done, 1)
                if kk == H:
                    pe.wait_ge(neg_done, 4 * H)
                if kk >= H:
                    out_first(S_AO, oT_hi, oT_lo, oTl_done, range(2 * (kk - H), 2 * (kk - H) + 2))
                if 2 <= kk < H + 2:
                    h = k - 2
                    for s in range(NB):
                        if s == 0:
                            pe.wait_ge(ptl_done, 3 * h + 3)
                        if s == 0 and kk == 2:
                            pe.wait_ge(c_l, 1)
                        if s == 0 and kk >= 3:
                            pe.wait_ge(ol_done, h)
                        c0 = (0, 4, 7, 9)[s] * P
                        n = (NB - s) * P
                        last = mm3(ps[:, 6, s * P:T], c_hi[:, s, :], c_lo[:, s, :],
                                   pt_hi[:, par, c0:c0 + n], pt_lo[:, par, c0:c0 + n], s == 0, s == NB - 1)
                    last.then_inc(o_done, 1)
                if 3 <= kk < H + 3:
                    h, p1 = k - 3, 1 - par
                    pe.wait_ge(ol_done, h + 1)
                    pe.wait_ge(uvl_done, h + 1)
                    if kk == 3:
                        pe.wait_ge(qa_done, H + 2)
                    if p1 == 0 and kk >= 5:
                        pe.wait_ge(oTl_done, (kk - 3) // 2 + it)
                    mm3(ps[:, 7, :], uv_hi[:, p1, :], uv_lo[:, p1, :], o_hi[:, p1, :], o_lo[:, p1, :],
                        p1 == 0, p1 == 1).then_inc(uv_done, 1)

            for kk in range(4):
                step(kk)
                if kk == 1:
                    pe.wait_ge(c_l, 1)
                    tile(ps[:, 7, :], S_A2 + 7, 0, P, 256, xh, xl)
            with pe.Fori(0, 5) as i:
                step(4, i)
                step(5, i)
            for kk in range(14, H + 3):
                step(kk)
            out_first(S_AO, oT_hi, oT_lo, oTl_done, range(6, DM))

            def feed_forward(layer, e, s_gu, s_d):
                def ff_tile(j, it=0):
                    for v in range(2):
                        if j >= 2:
                            pe.wait_ge((gate_done, up_done)[v], FT * layer + j - 1 + 2 * it)
                        tile(ps[:, 2 * (j % 2) + v, :], s_gu + j, it, v * P, 256, xh, xl)

                pe.wait_ge(x_new, DM * e + 6)
                first_tiles((ps[:, 0, :], ps[:, 1, :]), s_gu, e)
                norm_sum(e)
                ff_tile(1)
                with pe.Fori(0, (FT - 2) // 2) as i:
                    ff_tile(2, i)
                    ff_tile(3, i)

                def down_tile(m, it):
                    pe.wait_ge(x_new, DM * (e + 1) + m - 1 + 2 * it)
                    for c in range(2):
                        pe.wait_ge(al_done, FT * layer + KD * (c + 1))
                        tile(ps[:, 4 + m % 2, :], s_d + 2 * m + c, 2 * it, 0, P,
                             lambda k: act_hi[:, k, :], lambda k: act_lo[:, k, :],
                             k0=c * KD, nk=KD, start=c == 0, stop=c == 1)

                def y_turn(m, it):
                    pe.wait_ge(y_done, m + 2 * it + 1)
                    pe.wait_ge(y_copied, m + 2 * it + 1)
                    for t in range(NB):
                        last = nc.tensor.transpose(ps[:, m % 2, t * P:(t + 1) * P],
                                                   y_t[:, m % 2, t * P:(t + 1) * P], ident)
                    last.then_inc(y_tr, 1)

                if layer == 0:
                    with pe.Fori(0, DM // 2) as i:
                        for v in range(2):
                            down_tile(v, i)
                else:
                    down_tile(0, 0)
                    with pe.Fori(0, DM // 2 - 1) as i:
                        for v in range(2):
                            down_tile(1 + v, i)
                            y_turn(v, i)
                    down_tile(DM - 1, 0)
                    y_turn(DM - 2, 0)
                    y_turn(DM - 1, 0)

            out_rest(S_AO, 1, oT_hi, oT_lo)
            feed_forward(0, 1, S_F0, S_D0)
            first_tiles((ps[:, 0, :], ps[:, 1, :]), S_BK, 2)
            norm_sum(2)
            for u in range(2):
                tile(ps[:, 2 + u, :], S_BQ, 0, u * P, 256, xh, xl)
            pe.wait_ge(kvb_done, 2)
            for s in range(NB):
                last = nc.tensor.transpose(ps[:, 7, s * P:(s + 1) * P], kv[:, 1, s * P:(s + 1) * P], ident)
            last.then_inc(v_tr, 1)

            def b_project(u):
                n = S_BQ + u // 2
                pe.wait_ge(bqr_done, u)
                pe.wait_ge(lo_done, 2 * n + 2)
                for k in range(DM):
                    c = k * 256 + (u % 2) * P
                    last = mm3(ps[:, 4, :], w_hi[:, n % 2, c:c + P], w_lo[:, n % 2, c:c + P],
                               xh(k), xl(k), k == 0, k == DM - 1)
                last.then_inc(unit_done, 1)

            def b_turn(h2, a, k):
                par = k % 2
                for b in range(2):
                    pe.wait_ge(bnrm_done, 4 * (2 * h2 + a) + 3 + b)
                    if k >= 3 or a == 1:
                        pe.wait_ge(bptl_done, 4 * h2 + 2 * a - 1 + b)
                    for s in (2 * b, 2 * b + 1):
                        c0 = (s % 2) * 2 * P
                        own = OFFB[s] + (P if s else 0)
                        last = nc.tensor.transpose(ps[:, 5 + b, c0:c0 + P], b_prob[:, par, a, own:own + P], ident)
                        if s < NB - 1:
                            nxt = OFFB[s + 1]
                            last = nc.tensor.transpose(ps[:, 5 + b, c0 + P:c0 + 2 * P],
                                                       b_prob[:, par, a, nxt:nxt + P], ident)
                    last.then_inc(bpt_done, 1)

            b_project(2)
            pe.wait_ge(bkl_done, 1)
            pe.wait_ge(bqr_done, 2)

            def b_step(k):
                par = k % 2
                if 2 <= k < DM + 2:
                    h2 = k - 2
                    b_turn(h2, 0, k)
                for a in range(2):
                    if k < DM:
                        if a == 0:
                            pe.wait_ge(bql_done, k + 1)
                        r = slice(a * DH, (a + 1) * DH)
                        for b in range(2):
                            if k >= 1:
                                pe.wait_ge(bneg_done, 8 * (k - 1) + 4 * a + 2 * b + 2)
                            for i in (2 * b, 2 * b + 1):
                                n = P if i == 0 else 2 * P
                                c0 = (0, P, 0, 2 * P)[i]
                                k0 = max(i - 1, 0) * P
                                last = mm3(ps[:, 2 * a + b, c0:c0 + n], bq_hi[r, par, i * P:(i + 1) * P],
                                           bq_lo[r, par, i * P:(i + 1) * P], bk_hi[r, k0:k0 + n],
                                           bk_lo[r, k0:k0 + n], True, True)
                            last.then_inc(blg_done, 1)
                if 2 <= k < DM + 2:
                    b_turn(h2, 1, k)
                if k in Q_OF_STEP:
                    b_project(Q_OF_STEP[k])
                if k == DM:
                    pe.wait_ge(bneg_done, 8 * DM)
                if k >= DM:
                    out_first(S_BO, bo_hi, bo_lo, bol_done, range(2 * (k - DM) + 2, 2 * (k - DM) + 4))
                if 2 <= k < DM + 2:
                    for a in range(2):
                        for s in range(NB):
                            if s % 2 == 0:
                                pe.wait_ge(bptl_done, 4 * h2 + 2 * a + s // 2 + 1)
                            if a == 0 and s == 0 and k == 2:
                                pe.wait_ge(vl_done, 2)
                            if a == 0 and s == 0 and k >= 3:
                                pe.wait_ge(bol_done, h2)
                            n = 2 * P if s < NB - 1 else P
                            last = mm3(ps[:, 7, s * P:s * P + n], v_hi[:, a, s, :], v_lo[:, a, s, :],
                                       bpt_hi[:, a, s * 2 * P:s * 2 * P + n], bpt_lo[:, a, s * 2 * P:s * 2 * P + n],
                                       a == 0 and s == 0, a == 1 and s == NB - 1, skip_group_check=True)
                    last.then_inc(bo_done, 1)

            for k in range(DM + 2):
                b_step(k)
                if k == DM - 1:
                    pe.wait_ge(bneg_done, 8 * DM - 4)
                    out_first(S_BO, bo_hi, bo_lo, bol_done, range(0, 2))
            out_first(S_BO, bo_hi, bo_lo, bol_done, range(6, DM))
            out_rest(S_BO, 3, bo_hi, bo_lo)
            feed_forward(1, 3, S_F1, S_D1)
            pe.wait_ge(ss_done, DM * 5)
            for t in range(NB):
                last = nc.tensor.matmul(ps[:, 6, t:t + 1], ss[:, t * P:(t + 1) * P], ones[:, 0:1],
                                        start=True, stop=True)
            last.then_inc(ss_sum, 1)

        @block.scalar
        def _(act):
            def split_hi(n, it=0, after=0):
                for half in range(2):
                    split_half(n, half, it, after)

            def split_half(n, half, it=0, after=0):
                if half == 0:
                    act.wait_ge(raw_full[n % 2], 32 * (n // 2 + 1) + 32 * it)
                    if n >= 2:
                        act.wait_ge(unit_done, after)
                nc.scalar.copy(pieces(w_hi, n)[half], pieces(raw, n)[half]).then_inc(hi_done, 1)

            def split_after(m, it=0):
                split_hi(m + 2, it, units_through(m) + (1 if is_down(m) else 2) * 2 * it)

            def new_x(e, m, par, gain=None):
                c = DM * e + m
                n0 = held(act, c + 1)
                n1 = held(act, c - 1)
                act.wait_ge(tab_in, TAB)
                act.wait_ge(x_new, n0)
                if gain is not None:
                    nc.scalar.activation(xs_hi_m(m), x[:, m, :], ACT.Copy,
                                         scale=params[:, bass.ds(gain + m, 1)]).then_inc(xhi_done, 1)
                if e > 0 or m >= 2:
                    act.wait_ge(tab_in, TAB)
                    act.wait_ge(ss_done, n1)
                nc.scalar.activation(sq[:, par, :], x[:, m, :], ACT.Square).then_inc(sq_done, 1)

            def xs_hi_m(m):
                return xs_hi[:, bass.ds(m * T, T)]

            def norm(e):
                act.wait_ge(ss_sum, e + 1)
                nc.scalar.activation(std[:, :], ps[:, 6, :], ACT.Sqrt, bias=eps[:, 0:1], scale=1.0 / D)\
                    .then_inc(std_done, 1)

            def load_table(func):
                nc.scalar.activation(spare[:, 0:1], eps[:, :], func)

            for t in (1, 3):
                act.dma_start(x_tok[:, t, :], x_in[0, t * P:(t + 1) * P, :]).then_inc(x_in_s, 16)
                if t == 1:
                    act.dma_start(par_rows, par_in).then_inc(small_in, 16)
            act.dma_start(hot, consts[0:BUCKETS, C_HOT:C_END]).then_inc(hot_in, 16)
            act.dma_start(rel_sb, rel_bias).then_inc(hot_in, 16)
            act.wait_ge(set_up, 4)
            load_table(ACT.Sqrt)
            act.wait_ge(par_done, 1)
            for m in range(DM):
                act.wait_ge(x_new, m + 1)
                nc.scalar.activation(xs_hi_m(m), x[:, m, :], ACT.Copy,
                                     scale=params[:, GAIN[0] + m:GAIN[0] + m + 1]).then_inc(xhi_done, 1)
                if m in (1, 3):
                    split_half(0, m // 2)
            split_hi(1)
            for m in range(DM):
                nc.scalar.activation(sq_first[:, m, :], x[:, m, :], ACT.Square).then_inc(sq_done, 1)
            norm(0)
            split_after(0)
            act.wait_ge(ki_dup, 1)
            nc.scalar.copy(ki_hi, ps[:, 4, :]).then_inc(ki_h, 1)
            for u in range(2):
                act.wait_ge(unit_done, u + 3)
                nc.scalar.copy(qi_hi[:, u, :], ps[:, 2 + u, :]).then_inc(qi_h, 1)
            split_after(1)
            for u in range(2):
                act.wait_ge(unit_done, u + 5)
                nc.scalar.copy(qi_hi[:, 2 + u, :], ps[:, u, :]).then_inc(qi_h, 1)
            split_after(2)
            act.wait_ge(craw_done, 1)
            act.wait_ge(ss_done, DM)
            nc.scalar.activation(sq[:, 0, :], c_raw, ACT.Square).then_inc(csq_done, 1)
            act.wait_ge(row_out, 16)
            for i in range(1, NB):
                for j in range(JI):
                    d = (i - 1) * JI + j
                    act.wait_ge(dots, d + 1)
                    if d >= 4:
                        act.wait_ge(acc_done, d - 3)
                    nc.scalar.activation(relu[:, d % 4, 0:(i + 1) * P], ps[:, (d + 2) % 4, 0:(i + 1) * P],
                                         ACT.Relu).then_inc(relu_done, 1)
                if i == 2:
                    split_after(S_A2)
            act.wait_ge(css_sum, 1)
            nc.scalar.activation(std[:, :], ps[:, 6, :], ACT.Sqrt, bias=eps[:, 0:1], scale=1.0 / R)\
                .then_inc(cstd_done, 1)
            load_table(ACT.Exp)
            act.wait_ge(cn_done, 1)
            nc.scalar.copy(cT_hi[:, :], c_nrm).then_inc(cT_h, 1)
            act.wait_ge(c_tr, 1)
            nc.scalar.copy(c_hi[:, :, :].rearrange("p a b -> p (a b)"), ps[:, 7, :]).then_inc(c_h, 1)

            def q_head(h, par):
                n0 = held(act, 3 * (h - 1))
                act.wait_ge(tab_in, TAB)
                if not (isinstance(h, int) and h < 2):
                    act.wait_ge(lg_done, n0)
                act.wait_ge(qa_done, h + 3 if isinstance(h, int) else H + 2)
                nc.scalar.copy(q_hi[:, par, :], q_all[:, h, :]).then_inc(qh_done, 1)

            def uv_head(h, par, it):
                n0 = held(act, 16 * (it + 1))
                n1 = held(act, h - 1)
                act.wait_ge(tab_in, TAB)
                act.wait_ge(uv_full[par], n0)
                if not (isinstance(h, int) and h < 2):
                    act.wait_ge(uv_done, n1)
                nc.scalar.copy(uv_hi[:, par, par * DH:(par + 1) * DH], uv_raw[:, par, :]).then_inc(uvh_done, 1)

            def step(kk, it=0):
                k, par = kk + 2 * it, kk % 2
                if 2 <= kk < H + 2:
                    h = k - 2
                    for turn, (b, c0, n) in enumerate(((2, 7 * P, 3 * P), (1, 4 * P, 3 * P), (0, 0, 4 * P))):
                        act.wait_ge(pt_done, 3 * h + turn + 1)
                        nc.scalar.copy(pt_hi[:, par, c0:c0 + n], ps[:, 3 + b, 0:n]).then_inc(pth_done, 1)
                if 1 <= kk < H - 1:
                    q_head(k + 1, 1 - par)
                if 2 <= kk < H + 2:
                    uv_head(k - 2, par, (kk - 2) // 2 + it)
                if kk < H:
                    for i in range(NB):
                        n = (i + 1) * P
                        act.wait_ge(neg_done, 4 * k + i + 1)
                        nc.scalar.activation(prob[par][:, OFF[i]:OFF[i] + n], prob[par][:, OFF[i]:OFF[i] + n],
                                             ACT.Exp, bias=low[:, par, i:i + 1], scale=-1.0,
                                             accum_out=rsum[:, par, i:i + 1]).then_inc(exp_done, 1)
                if 2 <= kk < H + 2:
                    act.wait_ge(o_done, k - 1)
                    if kk >= 4:
                        act.wait_ge(uv_done, k - 3)
                    nc.scalar.copy(o_hi[:, par, :], ps[:, 6, :]).then_inc(oh_done, 1)
                if 3 <= kk < H + 3 and par == 0:
                    n0 = held(act, k - 2)
                    act.wait_ge(tab_in, TAB)
                    act.wait_ge(uv_done, n0)
                    nc.scalar.copy(oT_hi[:, (kk - 4) // 2 + it, :], ps[:, 7, :]).then_inc(oTh_done, 1)

            split_after(S_A2 + 1)
            q_head(0, 0)
            q_head(1, 1)
            with act.Fori(0, 2) as i:
                split_after(S_A2 + 2, i)
                split_after(S_A2 + 3, i)
            split_after(S_A2 + 6)
            for kk in range(4):
                step(kk)
            with act.Fori(0, 5) as i:
                step(4, i)
                step(5, i)
            for kk in range(14, H + 3):
                step(kk)
                if kk == H + 1:
                    split_after(S_A2 + 7)

            def out_proj(s0, e):
                with act.Fori(0, 2) as i:
                    for v in range(2):
                        split_after(s0 + v, i)
                        for u in range(2):
                            new_x(e, 2 * v + u + 4 * i, u, GAIN[e])

            def feed_forward(layer, e, s_gu, s_d):
                norm(e)
                load_table(ACT.Silu)

                def ff_tile(j, it=0):
                    split_after(s_gu + j, it)
                    t = FT * layer + j + 2 * it
                    act.wait_ge(gate_done, t + 1)
                    nc.scalar.activation(silu[:, :], gate[:, :], ACT.Silu).then_inc(silu_done, 1)
                    n0 = held(act, t + 1)
                    act.wait_ge(tab_in, TAB)
                    act.wait_ge(glu_done, n0)
                    nc.scalar.copy(act_hi[:, j + 2 * it, :], glu[:, j % 2, :]).then_inc(ah_done, 1)

                with act.Fori(0, (FT - 2) // 2) as i:
                    ff_tile(0, i)
                    ff_tile(1, i)
                ff_tile(FT - 2)
                ff_tile(FT - 1)
                load_table(ACT.Sqrt)

                def down_tile(m, it=0):
                    for c in range(2):
                        if s_d + 2 * m + c + 2 < S_END:
                            split_after(s_d + 2 * m + c, 2 * it)
                    if e + 1 < 4:
                        new_x(e + 1, m + 2 * it, m % 2, GAIN[e + 1])
                    else:
                        last_x(m, it)

                def last_x(m, it):
                    mm, par = m + 2 * it, m % 2
                    new_x(4, mm, par)
                    if m >= 2:
                        act.wait_ge(tab_in, TAB)
                        act.wait_ge(y_tr, mm - 1)
                    nc.scalar.activation(y_t[:, par, :], x[:, mm, :], ACT.Copy,
                                         scale=params[:, bass.ds(G_FINAL + mm, 1)]).then_inc(y_done, 1)
                    if m >= 1:
                        y_copy(mm - 1, 1 - par)

                if e + 1 < 4:
                    with act.Fori(0, (DM - 2) // 2) as i:
                        down_tile(0, i)
                        down_tile(1, i)
                else:
                    nc.scalar.copy(spare[:, 1:2], eps[:, :]).then_inc(y_copied, 2)
                    down_tile(0)
                    down_tile(1)
                    with act.Fori(0, (DM - 4) // 2) as i:
                        down_tile(2, i)
                        down_tile(3, i)
                down_tile(DM - 2)
                down_tile(DM - 1)

            def y_copy(m, par):
                n0 = held(act, m + 1)
                act.wait_ge(tab_in, TAB)
                act.wait_ge(y_tr, n0)
                nc.scalar.copy(y_tok[:, :, bass.ds(m * P, P)],
                               ps[:, par, :].rearrange("p (t c) -> p t c", t=NB)).then_inc(y_copied, 1)

            load_table(ACT.Sqrt)
            out_proj(S_AO, 1)
            feed_forward(0, 1, S_F0, S_D0)
            norm(2)
            load_table(ACT.Exp)
            split_after(S_BK)
            for a in range(2):
                act.wait_ge(kvr_done, a + 1)
                nc.scalar.activation(kv[:, a, :], bq_raw[:, a, :], ACT.Identity,
                                     bias=params[:, B_IN + 8 + a:B_IN + 9 + a]).then_inc(kvb_done, 1)
            act.wait_ge(kvb_done, 1)
            nc.scalar.copy(bk_hi[:, :], kv[:, 0, :]).then_inc(bkh_done, 1)
            act.wait_ge(nqb_done, 1)

            def b_bias(u):
                act.wait_ge(bqr_done, u + 1)
                nc.scalar.activation(bq_raw[:, u % 2, :], bq_raw[:, u % 2, :], ACT.Identity,
                                     bias=nq_bias[:, u:u + 1]).then_inc(bqa_done, 1)

            def b_q(j):
                if j >= 2:
                    act.wait_ge(blg_done, 4 * (j - 1))
                act.wait_ge(bqa_done, j + 1)
                nc.scalar.copy(bq_hi[:, j % 2, :], bq_raw[:, j % 2, :]).then_inc(bqh_done, 1)

            b_bias(0)
            b_q(0)
            b_bias(1)
            b_q(1)
            act.wait_ge(v_tr, 1)
            act.wait_ge(pad_done, 2)
            for a in range(2):
                nc.scalar.copy(v_hi[:, a, :, a * DH:(a + 1) * DH],
                               ps[:, 7, :].rearrange("p (s c) -> p s c", s=NB)[:, :, a * DH:(a + 1) * DH])\
                    .then_inc(vh_done, 1)
            split_after(S_BQ)
            b_bias(2)

            def b_step(k):
                par = k % 2
                for a in range(2):
                    if a == 1 and 2 <= k < DM - 1:
                        b_bias(k + 1)
                    if a == 1 and 1 <= k < DM - 1:
                        b_q(k + 1)
                    if 2 <= k < DM + 2:
                        h2 = k - 2
                        for b, n in enumerate((4 * P, 3 * P)):
                            act.wait_ge(bpt_done, 4 * h2 + 2 * a + b + 1)
                            if k >= 3:
                                act.wait_ge(bo_done, h2)
                            nc.scalar.copy(bpt_hi[:, a, b * 4 * P:b * 4 * P + n], ps[:, 5 + b, 0:n])\
                                .then_inc(bpth_done, 1)
                if k in (1, 4, 6):
                    split_after(S_BQ + (k + 1) // 2)
                for a in range(2):
                    if k < DM:
                        for i in range(NB):
                            n = P if i == 0 else 2 * P
                            at = b_prob[:, par, a, OFFB[i]:OFFB[i] + n]
                            act.wait_ge(bneg_done, 8 * k + 4 * a + i + 1)
                            nc.scalar.activation(at, at, ACT.Exp, bias=b_low[:, par, a, i:i + 1], scale=-1.0,
                                                 accum_out=b_rsum[:, par, a, i:i + 1])
                        nc.scalar.activation(b_sinkp[:, par, a, :], b_low[:, par, a, :], ACT.Exp,
                                             bias=sink2[:, par, a:a + 1]).then_inc(bsinkp_done, 1)
                if 2 <= k < DM + 2:
                    act.wait_ge(bo_done, k - 1)
                    nc.scalar.copy(bo_hi[:, k - 2, :], ps[:, 7, :]).then_inc(boh_done, 1)

            for k in range(DM + 2):
                b_step(k)
            load_table(ACT.Sqrt)
            out_proj(S_BO, 3)
            feed_forward(1, 3, S_F1, S_D1)
            act.wait_ge(ss_sum, 5)
            nc.scalar.activation(std[:, 0:NB], ps[:, 6, 0:NB], ACT.Sqrt, bias=eps[:, 0:1], scale=1.0 / D)\
                .then_inc(std_done, 1)
            y_copy(DM - 1, 1)
            act.wait_ge(rstd_done, 5)
            act.wait_ge(y_copied, DM + 2)
            for t in (1, 3):
                nc.scalar.activation(y_tok[:, t, :], y_tok[:, t, :], ACT.Copy, scale=rstd[:, t:t + 1])\
                    .then_inc(y_out[1], 1)

        @block.vector
        def _(dve):
            def lo_part(dst, src, hi, done):
                nc.vector.tensor_tensor(dst, src, hi, ALU.subtract).then_inc(done, 1)

            def new_x(e, m, par, gain=None):
                c = DM * e + m
                if gain is not None:
                    dve.wait_ge(xhi_done, c + 1)
                    nc.vector.scalar_tensor_tensor(xs_lo[:, bass.ds(m * T, T)], x[:, m, :],
                                                   params[:, bass.ds(gain + m, 1)],
                                                   xs_hi[:, bass.ds(m * T, T)].bitcast(F32),
                                                   ALU.mult, ALU.subtract).then_inc(xlo_done, 1)
                dve.wait_ge(sq_done, c + 1)
                if not (isinstance(c, int) and c == 0):
                    dve.wait_ge(ss_done, c)
                nc.vector.tensor_tensor(ss[:, :], ss[:, :], sq[:, par, :], ALU.add).then_inc(ss_done, 1)

            def norm(e):
                dve.wait_ge(std_done, e + 1)
                nc.vector.reciprocal(rstd[:, :], std[:, :]).then_inc(rstd_done, 1)
                nc.vector.memset(ss[:, :], 0.0).then_inc(ss_zero, 1)
                dve.wait_ge(rstd_done, e + 1)
                dve.wait_ge(ss_zero, e + 1)

            nc.vector.memset(rsum[:, :, :], 0.0).then_inc(qa_done, 2)
            nc.vector.memset(top8[:, :, :], 0.0).then_inc(topk, 1)
            dve.wait_ge(par_t, 1)
            nc.vector.tensor_copy(params[:, :], ps[:, 7, 0:59]).then_inc(par_done, 1)
            dve.wait_ge(par_done, 1)
            for m in range(DM + 1):
                if m < DM:
                    dve.wait_ge(x_tr, m + 1)
                    nc.vector.tensor_copy(x[:, m, :], ps[:, m % 4, :]).then_inc(x_new, 1)
                if m >= 1:
                    dve.wait_ge(xhi_done, m)
                    nc.vector.scalar_tensor_tensor(xs_lo[:, (m - 1) * T:m * T], x[:, m - 1, :],
                                                   params[:, GAIN[0] + m - 1:GAIN[0] + m],
                                                   xs_hi[:, (m - 1) * T:m * T].bitcast(F32),
                                                   ALU.mult, ALU.subtract).then_inc(xlo_done, 1)
            dve.wait_ge(g_mm, 2)
            nc.vector.tensor_copy(g_sb[:, 0:T], ps[0:H, 5, :]).then_inc(g_done, 1)
            nc.vector.tensor_copy(g_sb[:, T:GLEN], ps[0:H, 4, 0:GLEN - T]).then_inc(g_done, 1)
            dve.wait_ge(set_up, 3)
            for m in range(DM):
                dve.wait_ge(sq_done, m + 1)
                if m:
                    dve.wait_ge(ss_done, m)
                nc.vector.tensor_tensor(ss[:, :], ss[:, :], sq_first[:, m, :], ALU.add).then_inc(ss_done, 1)
            norm(0)
            dve.wait_ge(unit_done, 1)
            nc.vector.tensor_tensor(kw[0:DH, :], ps[0:DH, 0, :], rstd[0:DH, :], ALU.mult).then_inc(kw_done, 1)
            nc.vector.tensor_copy(kw[DH:DH + JI, :], ps[DH:DH + JI, 0, :]).then_inc(kw_done, 1)
            dve.wait_ge(unit_done, 2)
            nc.vector.tensor_tensor(c_raw, ps[:, 1, :], rstd[:, :], ALU.mult).then_inc(craw_done, 1)
            dve.wait_ge(ki_h, 1)
            lo_part(ki_lo, ps[:, 4, :], ki_hi.bitcast(F32), ki_l)
            dve.wait_ge(w_tr, 1)
            nc.vector.tensor_copy(w_col[:, :, :].rearrange("p i j -> p (i j)"), ps[:, 7, JI:4 * JI])\
                .then_inc(w_done, 1)
            for u in range(4):
                dve.wait_ge(qi_h, u + 1)
                lo_part(qi_lo[:, u, :], ps[:, (2, 3, 0, 1)[u], :], qi_hi[:, u, :].bitcast(F32), qi_l)

            def q_scale(h, bank):
                dve.wait_ge(unit_done, U_A2 + 1 + h)
                nc.vector.scalar_tensor_tensor(q_all[:, h, :], ps[:, bank, :], -float(R) ** -0.5, rstd[:, :],
                                               ALU.mult, ALU.mult).then_inc(qa_done, 1)

            def topk_round(r):
                for i in range(1, NB):
                    n0 = held(dve, 6 * r + 1)
                    dve.wait_ge(acc_done, 3 * JI)
                    dve.wait_ge(topk, n0)
                    nc.vector.max(top8[:, i - 1, :], work[:, OFF[i] - P:OFF[i] - P + (i + 1) * P])\
                        .then_inc(topk, 1)
                for i in range(1, NB):
                    row = work[:, OFF[i] - P:OFF[i] - P + (i + 1) * P]
                    n0 = held(dve, 6 * r + 1 + i)
                    dve.wait_ge(acc_done, 3 * JI)
                    dve.wait_ge(topk, n0)
                    nc.vector.match_replace(out=row, in_to_replace=top8[:, i - 1, :], in_values=row,
                                            imm_value=TAKEN).then_inc(topk, 1)

            dve.wait_ge(w_done, 1)
            dve.wait_ge(acc_zero, 3)
            dve.wait_ge(row_out, 16)
            for i in range(1, NB):
                n = (i + 1) * P
                row = work[:, OFF[i] - P:OFF[i] - P + n]
                for j in range(JI):
                    d = (i - 1) * JI + j
                    dve.wait_ge(relu_done, d + 1)
                    if j:
                        dve.wait_ge(acc_done, d)
                    nc.vector.scalar_tensor_tensor(row, relu[:, d % 4, 0:n], w_col[:, i - 1, j:j + 1], row,
                                                   ALU.mult, ALU.add).then_inc(acc_done, 1)
                q_scale(i - 1, 4 + (i - 1) % 2)
            dve.wait_ge(cstd_done, 1)
            nc.vector.reciprocal(std[:, :], std[:, :]).then_inc(crstd_done, 1)
            dve.wait_ge(crstd_done, 1)
            nc.vector.scalar_tensor_tensor(c_nrm, c_raw, params[:, G_LAT:G_LAT + 1], std[:, :],
                                           ALU.mult, ALU.mult).then_inc(cn_done, 1)
            dve.wait_ge(cT_h, 1)
            lo_part(cT_lo[:, :], c_nrm, cT_hi[:, :].bitcast(F32), cT_l)
            dve.wait_ge(c_h, 1)
            lo_part(c_lo[:, :, :].rearrange("p a b -> p (a b)"), ps[:, 7, :],
                    c_hi[:, :, :].rearrange("p a b -> p (a b)").bitcast(F32), c_l)
            for r in range(4):
                topk_round(r)
            q_scale(3, 3)
            with dve.Fori(0, 2) as it:
                for v in range(4):
                    topk_round(4 * it + v + 4)
                    q_scale(4 * it + v + 4, v)
            topk_round(12)
            q_scale(12, 0)
            topk_round(13)
            topk_round(14)
            q_scale(13, 1)
            topk_round(15)
            q_scale(14, 2)
            dve.wait_ge(topk, 6 * TOPK // 8 + 1)
            for i in range(1, NB):
                row = work[:, OFF[i] - P:OFF[i] - P + (i + 1) * P]
                nc.vector.tensor_scalar(row, row, TAKEN / 2, BIG, ALU.is_ge, ALU.mult).then_inc(mask_done, 1)

            def step(kk, it=0):
                k, par = kk + 2 * it, kk % 2

                def normalise():
                    p1 = 1 - par
                    dve.wait_ge(exp_done, 4 * k)
                    nc.vector.reciprocal(rinv[:, p1, :], rsum[:, p1, :]).then_inc(rinv_done, 1)
                    for i in reversed(range(NB)):
                        n = (i + 1) * P
                        if i == NB - 1:
                            dve.wait_ge(rinv_done, k)
                        at = prob[p1][:, OFF[i]:OFF[i] + n]
                        nc.vector.tensor_scalar(at, at, rinv[:, p1, i:i + 1], None, ALU.mult)\
                            .then_inc(nrm_done, 1)

                if kk == 1:
                    normalise()
                if 2 <= kk < H + 2:
                    h = k - 2
                    for turn, (b, c0, n) in enumerate(((2, 7 * P, 3 * P), (1, 4 * P, 3 * P), (0, 0, 4 * P))):
                        dve.wait_ge(pth_done, 3 * h + turn + 1)
                        lo_part(pt_lo[:, par, c0:c0 + n], ps[:, 3 + b, 0:n],
                                pt_hi[:, par, c0:c0 + n].bitcast(F32), ptl_done)
                if kk < H:
                    for i in range(NB):
                        n = (i + 1) * P
                        b, c0 = ((0, 0), (0, P), (1, 0), (2, 0))[i]
                        n0 = held(dve, 3 * k + b + 1)
                        n1 = held(dve, 4 * k + i + 1)
                        dve.wait_ge(mask_done, 3)
                        dve.wait_ge(lg_done, n0)
                        dve.wait_ge(bias_done, n1)
                        nc.vector.tensor_tensor_reduce(
                            out=prob[par][:, OFF[i]:OFF[i] + n], in0=ps[:, b, c0:c0 + n],
                            in1=bm[:, OFF[i]:OFF[i] + n], scale=1.0, scalar=3e38, op0=ALU.add, op1=ALU.min,
                            accum_out=low[:, par, i:i + 1]).then_inc(neg_done, 1)
                if 2 <= kk < H + 1:
                    normalise()
                if 2 <= kk < H + 2:
                    dve.wait_ge(oh_done, k - 1)
                    lo_part(o_lo[:, par, :], ps[:, 6, :], o_hi[:, par, :].bitcast(F32), ol_done)
                if 3 <= kk < H + 3 and par == 0:
                    m = (kk - 4) // 2 + it
                    dve.wait_ge(oTh_done, m + 1)
                    lo_part(oT_lo[:, m, :], ps[:, 7, :], oT_hi[:, m, :].bitcast(F32), oTl_done)

            for kk in range(4):
                step(kk)
                if kk == 1:
                    q_scale(H - 1, 7)
            with dve.Fori(0, 5) as i:
                step(4, i)
                step(5, i)
            for kk in range(14, H + 3):
                step(kk)

            def out_proj(u0, e, bias):
                with dve.Fori(0, 2) as i:
                    for v in range(4):
                        m = v + 4 * i
                        dve.wait_ge(unit_done, u0 + 1 + m)
                        if bias is None:
                            nc.vector.tensor_tensor(x[:, m, :], ps[:, v, :], x[:, m, :], ALU.add)\
                                .then_inc(x_new, 1)
                        else:
                            nc.vector.scalar_tensor_tensor(x[:, m, :], ps[:, v, :],
                                                           params[:, bass.ds(bias + m, 1)], x[:, m, :],
                                                           ALU.add, ALU.add).then_inc(x_new, 1)
                        new_x(e, m, v % 2, GAIN[e])

            def feed_forward(layer, e, u_gu, u_d):
                norm(e)

                def ff_tile(v, it):
                    t = FT * layer + v + 2 * it
                    b = 2 * v
                    dve.wait_ge(unit_done, u_gu + 2 * v + 1 + 4 * it)
                    if not (layer == 0 and isinstance(t, int) and t == 0):
                        dve.wait_ge(silu_done, t)
                    nc.vector.tensor_tensor(gate[:, :], ps[:, b, :], rstd[:, :], ALU.mult).then_inc(gate_done, 1)
                    dve.wait_ge(unit_done, u_gu + 2 * v + 2 + 4 * it)
                    nc.vector.tensor_tensor(up[:, :], ps[:, b + 1, :], rstd[:, :], ALU.mult).then_inc(up_done, 1)
                    dve.wait_ge(silu_done, t + 1)
                    dve.wait_ge(up_done, t + 1)
                    nc.vector.tensor_tensor(glu[:, v, :], silu[:, :], up[:, :], ALU.mult).then_inc(glu_done, 1)
                    dve.wait_ge(ah_done, t + 1)
                    nc.vector.tensor_tensor(act_lo[:, v + 2 * it, :], glu[:, v, :],
                                            act_hi[:, v + 2 * it, :].bitcast(F32), ALU.subtract)\
                        .then_inc(al_done, 1)

                ff_tile(0, 0)
                ff_tile(1, 0)
                with dve.Fori(1, FT // 2) as i:
                    ff_tile(0, i)
                    ff_tile(1, i)
                with dve.Fori(0, DM // 2) as i:
                    for v in range(2):
                        m = v + 2 * i
                        dve.wait_ge(unit_done, u_d + 2 + 2 * m)
                        nc.vector.tensor_tensor(x[:, m, :], ps[:, 4 + v, :], x[:, m, :], ALU.add)\
                            .then_inc(x_new, 1)
                        new_x(e + 1, m, v, GAIN[e + 1] if e + 1 < 4 else None)

            out_proj(U_AO, 1, None)
            feed_forward(0, 1, U_F0, U_D0)
            norm(2)
            for a in range(2):
                dve.wait_ge(unit_done, U_BK + 1 + a)
                nc.vector.tensor_tensor(bq_raw[:, a, :], ps[:, a, :], rstd[:, :], ALU.mult).then_inc(kvr_done, 1)
            nc.vector.tensor_scalar(nq_bias[:, :], params[:, B_IN:B_IN + DM], -float(DH) ** -0.5, None, ALU.mult)\
                .then_inc(nqb_done, 1)
            dve.wait_ge(sink_in, 16)
            nc.vector.tensor_scalar(nsink[:, :], sink[:, :], -1.0, None, ALU.mult).then_inc(sink_done, 1)
            dve.wait_ge(kvb_done, 2)
            dve.wait_ge(bkh_done, 1)
            lo_part(bk_lo[:, :], kv[:, 0, :], bk_hi[:, :].bitcast(F32), bkl_done)

            def b_scale(u):
                dve.wait_ge(unit_done, U_BQ + 1 + u)
                if u < 2:
                    dve.wait_ge(kvb_done, u + 1)
                else:
                    dve.wait_ge(bql_done, u - 1)
                nc.vector.scalar_tensor_tensor(bq_raw[:, u % 2, :], ps[:, 2 + u if u < 2 else 4, :],
                                               -float(DH) ** -0.5, rstd[:, :], ALU.mult, ALU.mult)\
                    .then_inc(bqr_done, 1)

            b_scale(0)
            b_scale(1)
            dve.wait_ge(vh_done, 2)
            for a in range(2):
                lo_part(v_lo[:, a, :, a * DH:(a + 1) * DH],
                        ps[:, 7, :].rearrange("p (s c) -> p s c", s=NB)[:, :, a * DH:(a + 1) * DH],
                        v_hi[:, a, :, a * DH:(a + 1) * DH].bitcast(F32), vl_done)
            b_scale(2)

            def b_step(k):
                par = k % 2
                if k < DM:
                    if k == 0:
                        dve.wait_ge(sink_done, 1)
                    for a in range(2):
                        j = k + a * (H // 2)
                        if k >= 2:
                            dve.wait_ge(bsinkp_done, 2 * (k - 1))
                        for two, one in ((sink2, sink), (nsink2, nsink)):
                            nc.vector.tensor_copy(two[:, par, a:a + 1], one[:, bass.ds(j, 1)])\
                                .then_inc(bsink2_done, 1)

                def lo_heads(a):
                    for b, n in enumerate((4 * P, 3 * P)):
                        c0 = b * 4 * P
                        dve.wait_ge(bpth_done, 4 * (k - 2) + 2 * a + b + 1)
                        lo_part(bpt_lo[:, a, c0:c0 + n], ps[:, 5 + b, 0:n],
                                bpt_hi[:, a, c0:c0 + n].bitcast(F32), bptl_done)

                if 2 <= k < DM + 2:
                    lo_heads(0)
                for a in range(2):
                    if k < DM:
                        for i in range(NB):
                            n = P if i == 0 else 2 * P
                            c0 = (0, P, 0, 2 * P)[i]
                            dve.wait_ge(blg_done, 4 * k + 2 * a + i // 2 + 1)
                            dve.wait_ge(bbias_done, 2 * k + a + 1)
                            dve.wait_ge(bsink2_done, 4 * k + 4)
                            if k >= 2:
                                dve.wait_ge(bpt_done, 4 * (k - 2) + 2 * a + 2)
                            nc.vector.tensor_tensor_reduce(
                                out=b_prob[:, par, a, OFFB[i]:OFFB[i] + n], in0=ps[:, 2 * a + i // 2, c0:c0 + n],
                                in1=b_bm[:, par, a, 2 * P - n:2 * P], scale=1.0, scalar=nsink2[:, par, a:a + 1],
                                op0=ALU.add, op1=ALU.min, accum_out=b_low[:, par, a, i:i + 1])\
                                .then_inc(bneg_done, 1)
                if 2 <= k < DM + 2:
                    lo_heads(1)
                for a in range(2):
                    if 1 <= k < DM + 1:
                        p1 = 1 - par
                        dve.wait_ge(bsinkp_done, 2 * k - 1 + a)
                        nc.vector.tensor_tensor(b_rsum[:, p1, a, :], b_rsum[:, p1, a, :], b_sinkp[:, p1, a, :],
                                                ALU.add).then_inc(brs_done, 1)
                        dve.wait_ge(brs_done, 2 * k - 1 + a)
                        nc.vector.reciprocal(b_rinv[:, p1, a, :], b_rsum[:, p1, a, :]).then_inc(brinv_done, 1)
                        for i in range(NB):
                            n = P if i == 0 else 2 * P
                            if i == 0:
                                dve.wait_ge(brinv_done, 2 * k - 1 + a)
                            at = b_prob[:, p1, a, OFFB[i]:OFFB[i] + n]
                            nc.vector.tensor_scalar(at, at, b_rinv[:, p1, a, i:i + 1], None, ALU.mult)\
                                .then_inc(bnrm_done, 1)
                if k in Q_OF_STEP:
                    b_scale(Q_OF_STEP[k])
                if 2 <= k < DM + 2:
                    dve.wait_ge(boh_done, k - 1)
                    lo_part(bo_lo[:, k - 2, :], ps[:, 7, :], bo_hi[:, k - 2, :].bitcast(F32), bol_done)

            for k in range(DM + 2):
                b_step(k)
            out_proj(U_BO, 3, B_OUT)
            feed_forward(1, 3, U_F1, U_D1)
            dve.wait_ge(std_done, 5)
            nc.vector.reciprocal(rstd[:, 0:NB], std[:, 0:NB]).then_inc(rstd_done, 1)
            dve.wait_ge(rstd_done, 5)
            dve.wait_ge(y_copied, DM + 2)
            for t in (0, 2):
                nc.vector.tensor_scalar(y_tok[:, t, :], y_tok[:, t, :], rstd[:, t:t + 1], None, ALU.mult)\
                    .then_inc(y_out[0], 1)


_INS = ['x', 'rel_bias', 'parameter_rows', 'a_w_in', 'a_w_uv', 'a_w_out', 'b_w_in', 'b_sinks', 'b_w_out',
        'ffn_w_gate_up', 'ffn_w_down']


def parameter_rows(attn_norm, ffn_norm, final_norm, a_latent_norm, b_b_in, b_b_out):
    q_bias = b_b_in[0, :D].reshape(2, DM, DH).swapaxes(0, 1)
    return np.concatenate([np.reshape(v, (-1, P)) for v in
                           (attn_norm, ffn_norm, final_norm, q_bias, b_b_in[0, D:], b_b_out, a_latent_norm)])


def kernel(**inputs):
    import concourse.bacc as _bacc
    from concourse.bass_utils import run_bass_kernel_spmd as _run

    nc = _bacc.Bacc("TRN2", target_bir_lowering=False, num_devices=1)
    arrays, args = {}, []
    inputs['parameter_rows'] = parameter_rows(**{n: np.asarray(inputs[n]) for n in (
        'attn_norm', 'ffn_norm', 'final_norm', 'a_latent_norm', 'b_b_in', 'b_b_out')})
    for name in _INS:
        a = np.ascontiguousarray(inputs[name])
        arrays[f"in_{name}"] = a
        args.append(nc.dram_tensor(f"in_{name}", a.shape, F32, kind="ExternalInput").ap())
    arrays["in_tables"] = tables()
    args.append(nc.dram_tensor("in_tables", (P, C_END), F32, kind="ExternalInput").ap())
    args.append(nc.dram_tensor("bias_row", (H, GLEN), F32, kind="Internal").ap())
    args.append(nc.dram_tensor("bias_toep", (H, P, T), F32, kind="Internal").ap())
    args.append(nc.dram_tensor("out_x", (1, T, D), F32, kind="ExternalOutput").ap())
    trunk(nc, *args)
    r = _run(nc, [arrays], core_ids=[0])
    return r.results[0]["out_x"]
```
